# Optimizing a Trainium2 kernel written in Bass

```python
import jax, jax.numpy as jnp
from jax import lax
import numpy as np
import math

D_MODEL = 1024
BATCH = 1
SEQ = 256
DEPTH = 2

N_MIXERS = 4
Q_BLOCK = 128
GATHER_CHUNK = 16
MAX_POS_OFFSET = 4096

MLA_HEADS = 8
MLA_NOPE = 128
MLA_ROPE = 64
MLA_V = 128
MLA_Q_RANK = 256
MLA_KV_RANK = 256
ROPE_BASE = 10000.0

MOBA_HEADS = 8
MOBA_HD = 128
MOBA_BLOCK = 256
MOBA_TOPK = 3

NSA_HEADS = 8
NSA_GROUPS = 2
NSA_HD = 128
NSA_CMP_LEN = 32
NSA_CMP_STRIDE = 16
NSA_SEL_BLOCK = 64
NSA_SEL_TOPN = 16
NSA_WINDOW = 512
NSA_FORCE_BONUS = 100.0

SB_HEADS = 8
SB_HD = 128

D_FF = 2816
CONV_W = 3
LN_EPS = 1e-5
RMS_EPS = 1e-6
NEG = -1e30
TINY = 1e-30
DEEPNORM_ALPHA = (2 * DEPTH) ** 0.25
DEEPNORM_BETA = (8 * DEPTH) ** -0.25


def _count(kind):
    return len(range(kind, DEPTH, N_MIXERS))

def layer_norm(x, g, b):
    xf = x.astype(jnp.float32)
    mu = jnp.mean(xf, -1, keepdims=True)
    var = jnp.mean(jnp.square(xf - mu), -1, keepdims=True)
    return ((xf - mu) * lax.rsqrt(var + LN_EPS) * g.astype(jnp.float32) + b.astype(jnp.float32)).astype(x.dtype)

def rms_norm(x, g):
    xf = x.astype(jnp.float32)
    return (xf * lax.rsqrt(jnp.mean(jnp.square(xf), -1, keepdims=True) + RMS_EPS) * g.astype(jnp.float32)).astype(x.dtype)

def apply_rope(x, cos, sin):
    half = x.shape[-1] // 2
    x1 = x[..., :half].astype(jnp.float32)
    x2 = x[..., half:].astype(jnp.float32)
    return jnp.concatenate([x1 * cos - x2 * sin, x2 * cos + x1 * sin], -1).astype(x.dtype)

def alibi_slopes(n):
    return 2.0 ** (-8.0 * jnp.arange(1, n + 1, dtype=jnp.float32) / n)

def masked_softmax(s, mask):
    s = jnp.where(mask, s, NEG)
    p = jnp.where(mask, jnp.exp(s - jnp.max(s, -1, keepdims=True)), 0.0)
    return p / jnp.maximum(jnp.sum(p, -1, keepdims=True), TINY)

def split_heads3(proj, n_heads, hd):
    B, S, _ = proj.shape
    t = proj.reshape(B, S, 3, n_heads, hd).transpose(2, 0, 3, 1, 4)
    return t[0], t[1], t[2]

def merge_heads(o):
    B, H, S, D = o.shape
    return o.transpose(0, 2, 1, 3).reshape(B, S, H * D)

def causal_softmax_attention(q, k, v, scale):
    B, H, S, Dk = q.shape
    nqb = S // Q_BLOCK
    q_blocks = q.reshape(B, H, nqb, Q_BLOCK, Dk).transpose(2, 0, 1, 3, 4)
    k_idx = jnp.arange(S)

    def block(args):
        q_b, bi = args
        s = jnp.einsum('bhqd,bhkd->bhqk', q_b, k, preferred_element_type=jnp.float32) * scale
        q_idx = bi * Q_BLOCK + jnp.arange(Q_BLOCK)
        p = masked_softmax(s, k_idx[None, :] <= q_idx[:, None])
        return jnp.einsum('bhqk,bhkd->bhqd', p.astype(v.dtype), v)

    o = lax.map(block, (q_blocks, jnp.arange(nqb)))
    return o.transpose(1, 2, 0, 3, 4).reshape(B, H, S, v.shape[-1])

def mla_mixer(h, cos, sin, w_in, q_norm, w_uq, kv_norm, w_ukv, w_o):
    B, S, _ = h.shape
    H, DN, DR, DV = MLA_HEADS, MLA_NOPE, MLA_ROPE, MLA_V
    proj = h @ w_in
    c_q = rms_norm(proj[..., :MLA_Q_RANK], q_norm)
    c_kv = rms_norm(proj[..., MLA_Q_RANK:MLA_Q_RANK + MLA_KV_RANK], kv_norm)
    k_rope = apply_rope(proj[..., MLA_Q_RANK + MLA_KV_RANK:], cos, sin)
    q = (c_q @ w_uq).reshape(B, S, H, DN + DR).transpose(0, 2, 1, 3)
    q = jnp.concatenate([q[..., :DN], apply_rope(q[..., DN:], cos[:, None], sin[:, None])], -1)
    kv = (c_kv @ w_ukv).reshape(B, S, H, DN + DV).transpose(0, 2, 1, 3)
    k = jnp.concatenate([kv[..., :DN], jnp.broadcast_to(k_rope[:, None], (B, H, S, DR))], -1)
    v = kv[..., DN:]
    o = causal_softmax_attention(q, k, v, (DN + DR) ** -0.5)
    return merge_heads(o) @ w_o

def moba_mixer(h, positions, w_in, w_o):
    B, S, _ = h.shape
    H, D, BLK, C = MOBA_HEADS, MOBA_HD, MOBA_BLOCK, GATHER_CHUNK
    q, k, v = split_heads3(h @ w_in, H, D)
    nb = -(-S // BLK)
    pad = nb * BLK - S
    posf = positions.astype(jnp.float32)
    k_p = jnp.pad(k, ((0, 0), (0, 0), (0, pad), (0, 0)))
    v_p = jnp.pad(v, ((0, 0), (0, 0), (0, pad), (0, 0)))
    pos_p = jnp.pad(posf, ((0, 0), (0, pad)))
    k_blk = k_p.reshape(B, H, nb, BLK, D)
    v_blk = v_p.reshape(B, H, nb, BLK, D)
    pos_blk = pos_p.reshape(B, nb, BLK)
    k_mean = jnp.mean(k_blk.astype(jnp.float32), axis=3)
    slope = alibi_slopes(H)[None, :, None, None]
    kk = min(MOBA_TOPK, nb)
    nch = S // C
    scale = D ** -0.5
    b_ix = jnp.arange(B)[:, None, None, None]
    h_ix = jnp.arange(H)[None, :, None, None]
    blk_off = jnp.arange(BLK)
    sel_rank = jnp.arange(kk)

    def chunk(args):
        q_c, pq, ci = args
        start = ci * C
        q_idx = start + jnp.arange(C)
        own = start // BLK
        gate = jnp.einsum('bhqd,bhnd->bhqn', q_c.astype(jnp.float32), k_mean)
        gate = jnp.where(jnp.arange(nb) < own, gate, NEG)
        _, sel = lax.top_k(gate, kk)
        sel_valid = sel_rank < own
        k_sel = k_blk[b_ix, h_ix, sel]
        v_sel = v_blk[b_ix, h_ix, sel]
        kpos_sel = pos_blk[b_ix, sel]
        s_sel = jnp.einsum('bhqd,bhqnkd->bhqnk', q_c, k_sel, preferred_element_type=jnp.float32) * scale
        s_sel = s_sel - slope[..., None] * jnp.abs(pq[:, None, :, None, None] - kpos_sel)
        k_own = lax.dynamic_slice_in_dim(k_p, own * BLK, BLK, axis=2)
        v_own = lax.dynamic_slice_in_dim(v_p, own * BLK, BLK, axis=2)
        kpos_own = lax.dynamic_slice_in_dim(pos_p, own * BLK, BLK, axis=1)
        s_own = jnp.einsum('bhqd,bhkd->bhqk', q_c, k_own, preferred_element_type=jnp.float32) * scale
        s_own = s_own - slope * jnp.abs(pq[:, None, :, None] - kpos_own[:, None, None, :])
        mask_own = (own * BLK + blk_off)[None, :] <= q_idx[:, None]
        mask_sel = jnp.broadcast_to(jnp.repeat(sel_valid, BLK)[None, :], (C, kk * BLK))
        s = jnp.concatenate([s_sel.reshape(B, H, C, kk * BLK), s_own], -1)
        p = masked_softmax(s, jnp.concatenate([mask_sel, mask_own], -1))
        p_sel = p[..., :kk * BLK].reshape(B, H, C, kk, BLK).astype(v.dtype)
        p_own = p[..., kk * BLK:].astype(v.dtype)
        return (jnp.einsum('bhqnk,bhqnkd->bhqd', p_sel, v_sel)
                + jnp.einsum('bhqk,bhkd->bhqd', p_own, v_own))

    q_chunks = q.reshape(B, H, nch, C, D).transpose(2, 0, 1, 3, 4)
    pq_chunks = posf.reshape(B, nch, C).transpose(1, 0, 2)
    o = lax.map(chunk, (q_chunks, pq_chunks, jnp.arange(nch)))
    o = o.transpose(1, 2, 0, 3, 4).reshape(B, H, S, D)
    return merge_heads(o) @ w_o

def nsa_mixer(h, positions, w_in, cmp_pos, cmp_w1, cmp_w2, w_o):
    B, S, _ = h.shape
    H, G, D = NSA_HEADS, NSA_GROUPS, NSA_HD
    R = H // G
    L, ST, SB, W = NSA_CMP_LEN, NSA_CMP_STRIDE, NSA_SEL_BLOCK, NSA_WINDOW
    proj = h @ w_in
    q = proj[..., :H * D].reshape(B, S, G, R, D).transpose(0, 2, 3, 1, 4)
    kv = proj[..., H * D:H * D + 6 * G * D].reshape(B, S, 6, G, D).transpose(2, 0, 3, 1, 4)
    k_cmp_raw, v_cmp_raw, k_slc, v_slc, k_win, v_win = kv[0], kv[1], kv[2], kv[3], kv[4], kv[5]
    gates = jax.nn.sigmoid(proj[..., H * D + 6 * G * D:].astype(jnp.float32))
    gates = gates.reshape(B, S, 3, G, R).transpose(2, 0, 3, 4, 1)[..., None]
    posf = positions.astype(jnp.float32)
    slope = alibi_slopes(H).reshape(G, R)[None, :, :, None, None]
    scale = D ** -0.5
    q_idx_all = jnp.arange(S)

    nc = (S - L) // ST + 1
    c_start = jnp.arange(nc) * ST
    c_idx = c_start[:, None] + jnp.arange(L)[None, :]
    c_end = c_start + L - 1

    def compress(t, pe, w1, w2):
        blocks = t[:, :, c_idx] + pe
        return jax.nn.gelu(blocks.reshape(B, G, nc, L * D) @ w1) @ w2

    k_c = compress(k_cmp_raw, cmp_pos[0], cmp_w1[0], cmp_w2[0])
    v_c = compress(v_cmp_raw, cmp_pos[1], cmp_w1[1], cmp_w2[1])
    s_c = jnp.einsum('bgrqd,bgnd->bgrqn', q, k_c, preferred_element_type=jnp.float32) * scale
    s_c = s_c - slope * jnp.abs(posf[:, None, None, :, None] - posf[:, c_end][:, None, None, None, :])
    p_c = masked_softmax(s_c, c_end[None, :] <= q_idx_all[:, None])
    o_cmp = jnp.einsum('bgrqn,bgnd->bgrqd', p_c.astype(v_c.dtype), v_c)

    ns = S // SB
    j_start = jnp.arange(ns) * SB
    overlap = ((c_start[:, None] < j_start[None, :] + SB) & (c_end[:, None] >= j_start[None, :])).astype(jnp.float32)
    imp = jnp.einsum('bgrqn,nj->bgqj', p_c, overlap)
    q_blk = q_idx_all // SB
    jj = jnp.arange(ns)
    forced = ((jj[None, :] == 0) | (jj[None, :] == q_blk[:, None]) | (jj[None, :] == q_blk[:, None] - 1)).astype(jnp.float32)
    imp = jnp.where(jj[None, :] <= q_blk[:, None], imp + NSA_FORCE_BONUS * forced, NEG)
    topn = min(NSA_SEL_TOPN, ns)
    _, sel = lax.top_k(imp, topn)
    sel_valid = jnp.arange(topn)[None, :] <= q_blk[:, None]

    k_sb = k_slc.reshape(B, G, ns, SB, D)
    v_sb = v_slc.reshape(B, G, ns, SB, D)
    pos_sb = posf.reshape(B, ns, SB)
    C = GATHER_CHUNK
    nch = S // C
    b_ix = jnp.arange(B)[:, None, None, None]
    g_ix = jnp.arange(G)[None, :, None, None]
    sb_off = jnp.arange(SB)

    def sel_chunk(args):
        q_c, pq, sel_c, valid_c, ci = args
        q_i = ci * C + jnp.arange(C)
        k_g = k_sb[b_ix, g_ix, sel_c]
        v_g = v_sb[b_ix, g_ix, sel_c]
        kpos = pos_sb[b_ix, sel_c]
        k_i = sel_c[..., None] * SB + sb_off
        s = jnp.einsum('bgrqd,bgqnkd->bgrqnk', q_c, k_g, preferred_element_type=jnp.float32) * scale
        s = s - slope[..., None] * jnp.abs(pq[:, None, None, :, None, None] - kpos[:, :, None])
        mask = valid_c[None, None, :, :, None] & (k_i <= q_i[None, None, :, None, None])
        p = masked_softmax(s.reshape(B, G, R, C, topn * SB), mask.reshape(B, G, 1, C, topn * SB))
        return jnp.einsum('bgrqnk,bgqnkd->bgrqd', p.reshape(B, G, R, C, topn, SB).astype(v_g.dtype), v_g)

    o_sel = lax.map(sel_chunk, (
        q.reshape(B, G, R, nch, C, D).transpose(3, 0, 1, 2, 4, 5),
        posf.reshape(B, nch, C).transpose(1, 0, 2),
        sel.reshape(B, G, nch, C, topn).transpose(2, 0, 1, 3, 4),
        sel_valid.reshape(nch, C, topn),
        jnp.arange(nch)))
    o_sel = o_sel.transpose(1, 2, 3, 0, 4, 5).reshape(B, G, R, S, D)

    QB = Q_BLOCK
    nqb = S // QB
    span = W + QB
    band = jnp.arange(nqb)[:, None] * QB + jnp.arange(span)[None, :]
    k_w = jnp.pad(k_win, ((0, 0), (0, 0), (W, 0), (0, 0)))[:, :, band]
    v_w = jnp.pad(v_win, ((0, 0), (0, 0), (W, 0), (0, 0)))[:, :, band]
    kpos_w = jnp.pad(posf, ((0, 0), (W, 0)))[:, band]
    k_i = (band - W)[:, None, :]
    q_i = (jnp.arange(nqb)[:, None] * QB + jnp.arange(QB)[None, :])[:, :, None]
    mask_w = (k_i >= 0) & (k_i <= q_i) & (q_i - k_i < W)
    q_w = q.reshape(B, G, R, nqb, QB, D)
    s_w = jnp.einsum('bgriqd,bgikd->bgriqk', q_w, k_w, preferred_element_type=jnp.float32) * scale
    s_w = s_w - slope[..., None] * jnp.abs(posf.reshape(B, nqb, QB)[:, None, None, :, :, None] - kpos_w[:, None, None, :, None, :])
    p_w = masked_softmax(s_w, mask_w)
    o_win = jnp.einsum('bgriqk,bgikd->bgriqd', p_w.astype(v_w.dtype), v_w).reshape(B, G, R, S, D)

    o = gates[0] * o_cmp + gates[1] * o_sel + gates[2] * o_win
    o = o.transpose(0, 3, 1, 2, 4).reshape(B, S, H * D).astype(h.dtype)
    return o @ w_o

def stick_breaking_mixer(h, w_in, w_o):
    B, S, _ = h.shape
    H, D = SB_HEADS, SB_HD
    q, k, v = split_heads3(h @ w_in, H, D)
    scale = D ** -0.5
    nqb = S // Q_BLOCK
    k_idx = jnp.arange(S)

    def block(args):
        q_b, bi = args
        z = jnp.einsum('bhqd,bhkd->bhqk', q_b, k, preferred_element_type=jnp.float32) * scale
        q_idx = bi * Q_BLOCK + jnp.arange(Q_BLOCK)
        mask = k_idx[None, :] < q_idx[:, None]
        log_beta = jax.nn.log_sigmoid(z)
        log_1mb = jnp.where(mask, jax.nn.log_sigmoid(-z), 0.0)
        tail = lax.cumsum(log_1mb, axis=3, reverse=True) - log_1mb
        a = jnp.where(mask, jnp.exp(log_beta + tail), 0.0)
        return jnp.einsum('bhqk,bhkd->bhqd', a.astype(v.dtype), v)

    q_blocks = q.reshape(B, H, nqb, Q_BLOCK, D).transpose(2, 0, 1, 3, 4)
    o = lax.map(block, (q_blocks, jnp.arange(nqb)))
    o = o.transpose(1, 2, 0, 3, 4).reshape(B, H, S, D)
    return merge_heads(o) @ w_o

def conv_ffn(h, w_in, conv_w, conv_b, w_out):
    u = h @ w_in
    a, b = u[..., :D_FF], u[..., D_FF:]
    a = lax.conv_general_dilated(a, conv_w[:, None, :].astype(a.dtype), window_strides=(1,),
                                 padding=[(CONV_W - 1, 0)], dimension_numbers=('NWC', 'WIO', 'NWC'),
                                 feature_group_count=D_FF) + conv_b
    return (jax.nn.gelu(a) * b) @ w_out

def _w(key, shape, fan_in, scale=1.0):
    return jax.random.normal(key, shape, jnp.float32) * (scale * fan_in ** -0.5)

def _gain(key, shape):
    return 1.0 + 0.02 * jax.random.normal(key, shape, jnp.float32)

def _small(key, shape):
    return 0.02 * jax.random.normal(key, shape, jnp.float32)

def first_inputs(seed: int = 0) -> dict:
    key = jax.random.key(seed)
    ks = jax.random.split(key, 32)
    D = D_MODEL
    nA, nB, nC, nD = _count(0), _count(1), _count(2), _count(3)
    mla_out = MLA_Q_RANK + MLA_KV_RANK + MLA_ROPE
    nsa_out = NSA_HEADS * NSA_HD + 6 * NSA_GROUPS * NSA_HD + 3 * NSA_HEADS
    mod_base = jnp.repeat(jnp.array([0.0, 0.0, 1.0, 0.0, 0.0, 1.0], jnp.float32), D)
    offset = jax.random.randint(ks[2], (BATCH, 1), 0, MAX_POS_OFFSET, dtype=jnp.int32)
    return {
        'x': jax.random.normal(ks[0], (BATCH, SEQ, D), jnp.float32),
        'c': jax.random.normal(ks[1], (BATCH, D), jnp.float32),
        'positions': offset + jnp.arange(SEQ, dtype=jnp.int32)[None, :],
        'mod_w': _w(ks[3], (DEPTH, D, 6 * D), D, 0.1),
        'mod_b': mod_base + _small(ks[4], (DEPTH, 6 * D)),
        'ln_g': _gain(ks[5], (DEPTH, 2, D)),
        'ln_b': _small(ks[6], (DEPTH, 2, D)),
        'ffn_w_in': _w(ks[7], (DEPTH, D, 2 * D_FF), D),
        'ffn_conv_w': _w(ks[8], (DEPTH, CONV_W, D_FF), CONV_W),
        'ffn_conv_b': _small(ks[9], (DEPTH, D_FF)),
        'ffn_w_out': _w(ks[10], (DEPTH, D_FF, D), D_FF, DEEPNORM_BETA),
        'mla_w_in': _w(ks[11], (nA, D, mla_out), D),
        'mla_q_norm': _gain(ks[12], (nA, MLA_Q_RANK)),
        'mla_w_uq': _w(ks[13], (nA, MLA_Q_RANK, MLA_HEADS * (MLA_NOPE + MLA_ROPE)), MLA_Q_RANK),
        'mla_kv_norm': _gain(ks[14], (nA, MLA_KV_RANK)),
        'mla_w_ukv': _w(ks[15], (nA, MLA_KV_RANK, MLA_HEADS * (MLA_NOPE + MLA_V)), MLA_KV_RANK),
        'mla_w_o': _w(ks[16], (nA, MLA_HEADS * MLA_V, D), MLA_HEADS * MLA_V, DEEPNORM_BETA),
        'moba_w_in': _w(ks[17], (nB, D, 3 * MOBA_HEADS * MOBA_HD), D),
        'moba_w_o': _w(ks[18], (nB, MOBA_HEADS * MOBA_HD, D), MOBA_HEADS * MOBA_HD, DEEPNORM_BETA),
        'nsa_w_in': _w(ks[19], (nC, D, nsa_out), D),
        'nsa_cmp_pos': _small(ks[20], (nC, 2, NSA_CMP_LEN, NSA_HD)),
        'nsa_cmp_w1': _w(ks[21], (nC, 2, NSA_CMP_LEN * NSA_HD, NSA_HD), NSA_CMP_LEN * NSA_HD),
        'nsa_cmp_w2': _w(ks[22], (nC, 2, NSA_HD, NSA_HD), NSA_HD),
        'nsa_w_o': _w(ks[23], (nC, NSA_HEADS * NSA_HD, D), NSA_HEADS * NSA_HD, DEEPNORM_BETA),
        'sb_w_in': _w(ks[24], (nD, D, 3 * SB_HEADS * SB_HD), D),
        'sb_w_o': _w(ks[25], (nD, SB_HEADS * SB_HD, D), SB_HEADS * SB_HD, DEEPNORM_BETA),
    }

def first_block(x, c, positions, mod_w, mod_b, ln_g, ln_b, ffn_w_in, ffn_conv_w, ffn_conv_b, ffn_w_out,
              mla_w_in, mla_q_norm, mla_w_uq, mla_kv_norm, mla_w_ukv, mla_w_o,
              moba_w_in, moba_w_o, nsa_w_in, nsa_cmp_pos, nsa_cmp_w1, nsa_cmp_w2, nsa_w_o,
              sb_w_in, sb_w_o):
    B, S, D = x.shape
    half = MLA_ROPE // 2
    inv_freq = ROPE_BASE ** (-jnp.arange(half, dtype=jnp.float32) / half)
    ang = positions.astype(jnp.float32)[..., None] * inv_freq
    cos, sin = jnp.cos(ang), jnp.sin(ang)
    c_act = jax.nn.silu(c)
    for i in range(DEPTH):
        kind, j = i % N_MIXERS, i // N_MIXERS
        mod = (c_act @ mod_w[i] + mod_b[i]).reshape(B, 6, D)[:, :, None, :]
        hin = x * (1.0 + mod[:, 1]) + mod[:, 0]
        if kind == 0:
            y = mla_mixer(hin, cos, sin, mla_w_in[j], mla_q_norm[j], mla_w_uq[j], mla_kv_norm[j], mla_w_ukv[j], mla_w_o[j])
        elif kind == 1:
            y = moba_mixer(hin, positions, moba_w_in[j], moba_w_o[j])
        elif kind == 2:
            y = nsa_mixer(hin, positions, nsa_w_in[j], nsa_cmp_pos[j], nsa_cmp_w1[j], nsa_cmp_w2[j], nsa_w_o[j])
        else:
            y = stick_breaking_mixer(hin, sb_w_in[j], sb_w_o[j])
        x = layer_norm(DEEPNORM_ALPHA * x + mod[:, 2] * y, ln_g[i, 0], ln_b[i, 0])
        hin = x * (1.0 + mod[:, 4]) + mod[:, 3]
        y = conv_ffn(hin, ffn_w_in[i], ffn_conv_w[i], ffn_conv_b[i], ffn_w_out[i])
        x = layer_norm(DEEPNORM_ALPHA * x + mod[:, 5] * y, ln_g[i, 1], ln_b[i, 1])
    return x


HEAD_DIM = 64
A_Q_HEADS = 8
A_KV_HEADS = 2
A_GROUP = A_Q_HEADS // A_KV_HEADS
WINDOW = 128
BLOCK = 128
B_HEADS = 8
A_WIDTH = A_Q_HEADS * HEAD_DIM
A_KV_WIDTH = A_KV_HEADS * HEAD_DIM
B_WIDTH = B_HEADS * HEAD_DIM
ATTN_WIDTH = A_WIDTH + B_WIDTH
ATTN_SPLITS = (A_WIDTH, A_KV_WIDTH, A_KV_WIDTH, B_WIDTH, B_WIDTH, B_WIDTH, B_HEADS, ATTN_WIDTH)
ATTN_IN = sum(ATTN_SPLITS)
REL_BUCKETS = 32
REL_MAX_EXACT = 16
REL_MAX_DIST = 128
LRU_WIDTH = D_MODEL
LRU_BLOCKS = 8
LRU_BLOCK_W = LRU_WIDTH // LRU_BLOCKS
CONV_WIDTH = 4
LRU_C = 8.0
N_ATTN_LAYERS = (DEPTH + 1) // 2
N_LRU_LAYERS = DEPTH // 2
EPS = 1e-6


def rmsnorm(x, g):
    x32 = x.astype(jnp.float32)
    y = x32 * lax.rsqrt(jnp.mean(x32 * x32, axis=-1, keepdims=True) + EPS)
    return (y * g.astype(jnp.float32)).astype(x.dtype)

def t5_causal_bucket(rel):
    n = jnp.maximum(rel, 0)
    nf = jnp.maximum(n, 1).astype(jnp.float32)
    large = REL_MAX_EXACT + (jnp.log(nf / REL_MAX_EXACT) / math.log(REL_MAX_DIST / REL_MAX_EXACT)
                             * (REL_BUCKETS - REL_MAX_EXACT)).astype(jnp.int32)
    large = jnp.minimum(large, REL_BUCKETS - 1)
    return jnp.where(n < REL_MAX_EXACT, n, large)

def swa_sink_attention(q, k, v, sinks, rel_bias):
    B, S = q.shape[0], q.shape[1]
    nb = S // BLOCK
    qb = q.reshape(B, nb, BLOCK, A_KV_HEADS, A_GROUP, HEAD_DIM)
    pad = ((0, 0), (BLOCK, 0), (0, 0), (0, 0))
    kp = jnp.pad(k, pad)[:, :S].reshape(B, nb, BLOCK, A_KV_HEADS, HEAD_DIM)
    vp = jnp.pad(v, pad)[:, :S].reshape(B, nb, BLOCK, A_KV_HEADS, HEAD_DIM)
    kb = jnp.concatenate([kp, k.reshape(B, nb, BLOCK, A_KV_HEADS, HEAD_DIM)], axis=2)
    vb = jnp.concatenate([vp, v.reshape(B, nb, BLOCK, A_KV_HEADS, HEAD_DIM)], axis=2)
    scores = jnp.einsum('bnqhgd,bnkhd->bhgnqk', qb, kb).astype(jnp.float32) * (HEAD_DIM ** -0.5)
    qi = jnp.arange(BLOCK)[:, None]
    kj = jnp.arange(2 * BLOCK)[None, :]
    rel = qi - kj + BLOCK
    bias = rel_bias.astype(jnp.float32)[t5_causal_bucket(rel)]
    bias = jnp.transpose(bias, (2, 0, 1)).reshape(A_KV_HEADS, A_GROUP, 1, BLOCK, 2 * BLOCK)
    valid = (rel >= 0) & (rel < WINDOW)
    first = (jnp.arange(nb)[:, None, None] == 0) & (kj[None] < BLOCK)
    mask = valid[None] & ~first
    logits = jnp.where(mask, scores + bias, -jnp.inf)
    sink = jnp.broadcast_to(sinks.astype(jnp.float32).reshape(1, A_KV_HEADS, A_GROUP, 1, 1, 1),
                            logits.shape[:-1] + (1,))
    probs = jax.nn.softmax(jnp.concatenate([logits, sink], axis=-1), axis=-1)[..., :-1]
    out = jnp.einsum('bhgnqk,bnkhd->bnqhgd', probs.astype(v.dtype), vb)
    return out.reshape(B, S, A_WIDTH)

def forgetting_attention(q, k, v, log_f):
    B, S = q.shape[0], q.shape[1]
    nb = S // BLOCK
    F = jnp.cumsum(log_f, axis=1)
    outs = []
    for n in range(nb):
        q0, kend = n * BLOCK, (n + 1) * BLOCK
        qs = q[:, q0:kend]
        ks, vs = k[:, :kend], v[:, :kend]
        s = jnp.einsum('bqhd,bkhd->bhqk', qs, ks).astype(jnp.float32) * (HEAD_DIM ** -0.5)
        decay = jnp.transpose(F[:, q0:kend], (0, 2, 1))[..., :, None] - jnp.transpose(F[:, :kend], (0, 2, 1))[..., None, :]
        tpos = q0 + jnp.arange(BLOCK)[:, None]
        spos = jnp.arange(kend)[None, :]
        p = jax.nn.softmax(jnp.where(spos <= tpos, s + decay, -jnp.inf), axis=-1)
        outs.append(jnp.einsum('bhqk,bkhd->bqhd', p.astype(v.dtype), vs))
    return jnp.concatenate(outs, axis=1).reshape(B, S, B_WIDTH)

def attention_mixer(h, w_in, sinks, b_f, w_out, rel_bias):
    B, S, _ = h.shape
    proj = h @ w_in
    idx = np.cumsum(ATTN_SPLITS)[:-1].tolist()
    a_q, a_k, a_v, b_q, b_k, b_v, f_logit, gate = jnp.split(proj, idx, axis=-1)
    a_out = swa_sink_attention(a_q.reshape(B, S, A_Q_HEADS, HEAD_DIM),
                               a_k.reshape(B, S, A_KV_HEADS, HEAD_DIM),
                               a_v.reshape(B, S, A_KV_HEADS, HEAD_DIM), sinks, rel_bias)
    log_f = jax.nn.log_sigmoid((f_logit + b_f).astype(jnp.float32))
    b_out = forgetting_attention(b_q.reshape(B, S, B_HEADS, HEAD_DIM),
                                 b_k.reshape(B, S, B_HEADS, HEAD_DIM),
                                 b_v.reshape(B, S, B_HEADS, HEAD_DIM), log_f)
    y = jnp.concatenate([a_out, b_out], axis=-1) * jax.nn.silu(gate)
    return y @ w_out

def rglru_mixer(h, w_in, conv_w, conv_b, w_a, b_a, w_x, b_x, lam, w_out):
    B, S, _ = h.shape
    proj = h @ w_in
    xr, gate = proj[..., :LRU_WIDTH], proj[..., LRU_WIDTH:]
    xp = jnp.pad(xr, ((0, 0), (CONV_WIDTH - 1, 0), (0, 0)))
    xc = conv_b
    for j in range(CONV_WIDTH):
        xc = xc + xp[:, j:j + S] * conv_w[j]
    xblk = xc.reshape(B, S, LRU_BLOCKS, LRU_BLOCK_W)
    r = jax.nn.sigmoid((jnp.einsum('bsnw,nwv->bsnv', xblk, w_a).reshape(B, S, LRU_WIDTH) + b_a).astype(jnp.float32))
    i = jax.nn.sigmoid((jnp.einsum('bsnw,nwv->bsnv', xblk, w_x).reshape(B, S, LRU_WIDTH) + b_x).astype(jnp.float32))
    log_a = -LRU_C * r * jax.nn.softplus(-lam.astype(jnp.float32))
    a = jnp.exp(log_a)
    u = jnp.sqrt(-jnp.expm1(2.0 * log_a)) * (i * xc.astype(jnp.float32))

    def step(state, inp):
        a_t, u_t = inp
        state = a_t * state + u_t
        return state, state

    _, hs = lax.scan(step, jnp.zeros((B, LRU_WIDTH), jnp.float32),
                     (jnp.transpose(a, (1, 0, 2)), jnp.transpose(u, (1, 0, 2))))
    y = jnp.transpose(hs, (1, 0, 2)).astype(h.dtype) * jax.nn.silu(gate)
    return y @ w_out

def second_inputs(seed: int = 0) -> dict:
    key = jax.random.key(seed)
    ks = jax.random.split(key, 22)
    nrm = lambda k, shape, s: jax.random.normal(k, shape, jnp.float32) * s
    a0 = jax.random.uniform(ks[19], (N_LRU_LAYERS, LRU_WIDTH), jnp.float32, 0.9, 0.999) ** (1.0 / LRU_C)
    return {
        "x": nrm(ks[0], (BATCH, SEQ, D_MODEL), 1.0),
        "c": nrm(ks[1], (BATCH, D_MODEL), 1.0),
        "rel_bias": nrm(ks[2], (REL_BUCKETS, A_Q_HEADS), 0.2),
        "norm_g": 1.0 + nrm(ks[3], (DEPTH, D_MODEL), 0.05),
        "ada_w": nrm(ks[4], (DEPTH, D_MODEL, 3 * D_MODEL), 0.3 * D_MODEL ** -0.5),
        "ada_b": nrm(ks[5], (DEPTH, 3 * D_MODEL), 0.02),
        "attn_w_in": nrm(ks[6], (N_ATTN_LAYERS, D_MODEL, ATTN_IN), D_MODEL ** -0.5),
        "attn_sinks": nrm(ks[7], (N_ATTN_LAYERS, A_Q_HEADS), 0.5),
        "attn_b_f": jax.random.uniform(ks[8], (N_ATTN_LAYERS, B_HEADS), jnp.float32, 1.0, 4.0),
        "attn_w_out": nrm(ks[9], (N_ATTN_LAYERS, ATTN_WIDTH, D_MODEL), ATTN_WIDTH ** -0.5),
        "lru_w_in": nrm(ks[10], (N_LRU_LAYERS, D_MODEL, 2 * LRU_WIDTH), D_MODEL ** -0.5),
        "lru_conv_w": nrm(ks[11], (N_LRU_LAYERS, CONV_WIDTH, LRU_WIDTH), CONV_WIDTH ** -0.5),
        "lru_conv_b": nrm(ks[12], (N_LRU_LAYERS, LRU_WIDTH), 0.02),
        "lru_w_a": nrm(ks[13], (N_LRU_LAYERS, LRU_BLOCKS, LRU_BLOCK_W, LRU_BLOCK_W), LRU_BLOCK_W ** -0.5),
        "lru_b_a": nrm(ks[14], (N_LRU_LAYERS, LRU_WIDTH), 0.02),
        "lru_w_x": nrm(ks[15], (N_LRU_LAYERS, LRU_BLOCKS, LRU_BLOCK_W, LRU_BLOCK_W), LRU_BLOCK_W ** -0.5),
        "lru_b_x": nrm(ks[16], (N_LRU_LAYERS, LRU_WIDTH), 0.02),
        "lru_lambda": jnp.log(a0) - jnp.log1p(-a0),
        "lru_w_out": nrm(ks[17], (N_LRU_LAYERS, LRU_WIDTH, D_MODEL), LRU_WIDTH ** -0.5),
        "final_g": 1.0 + nrm(ks[18], (D_MODEL,), 0.05),
    }

def second_block(x, c, rel_bias, norm_g, ada_w, ada_b, attn_w_in, attn_sinks, attn_b_f, attn_w_out,
              lru_w_in, lru_conv_w, lru_conv_b, lru_w_a, lru_b_a, lru_w_x, lru_b_x, lru_lambda,
              lru_w_out, final_g):
    c_act = jax.nn.silu(c)
    for layer in range(DEPTH):
        mod = c_act @ ada_w[layer] + ada_b[layer]
        shift, scale, gate = jnp.split(mod, 3, axis=-1)
        h = rmsnorm(x, norm_g[layer]) * (1.0 + scale[:, None, :]) + shift[:, None, :]
        if layer % 2 == 0:
            j = layer // 2
            y = attention_mixer(h, attn_w_in[j], attn_sinks[j], attn_b_f[j], attn_w_out[j], rel_bias)
        else:
            j = layer // 2
            y = rglru_mixer(h, lru_w_in[j], lru_conv_w[j], lru_conv_b[j], lru_w_a[j], lru_b_a[j],
                            lru_w_x[j], lru_b_x[j], lru_lambda[j], lru_w_out[j])
        x = x + gate[:, None, :] * y
    return rmsnorm(x, final_g)


def setup_inputs(seed=0):
    out = dict(first_inputs(seed))
    for name, value in second_inputs(seed + 1).items():
        if name != "x":
            out[name + "_2"] = value
    return out


def reference(
    x, c, positions, mod_w, mod_b, ln_g, ln_b, ffn_w_in, ffn_conv_w, ffn_conv_b, ffn_w_out,
    mla_w_in, mla_q_norm, mla_w_uq, mla_kv_norm, mla_w_ukv, mla_w_o, moba_w_in, moba_w_o,
    nsa_w_in, nsa_cmp_pos, nsa_cmp_w1, nsa_cmp_w2, nsa_w_o, sb_w_in, sb_w_o, c_2, rel_bias_2,
    norm_g_2, ada_w_2, ada_b_2, attn_w_in_2, attn_sinks_2, attn_b_f_2, attn_w_out_2, lru_w_in_2,
    lru_conv_w_2, lru_conv_b_2, lru_w_a_2, lru_b_a_2, lru_w_x_2, lru_b_x_2, lru_lambda_2,
    lru_w_out_2, final_g_2,
):
    x = first_block(
        x, c, positions, mod_w, mod_b, ln_g, ln_b, ffn_w_in, ffn_conv_w, ffn_conv_b, ffn_w_out,
        mla_w_in, mla_q_norm, mla_w_uq, mla_kv_norm, mla_w_ukv, mla_w_o, moba_w_in, moba_w_o,
        nsa_w_in, nsa_cmp_pos, nsa_cmp_w1, nsa_cmp_w2, nsa_w_o, sb_w_in, sb_w_o,
    )
    return second_block(
        x, c_2, rel_bias_2, norm_g_2, ada_w_2, ada_b_2, attn_w_in_2, attn_sinks_2, attn_b_f_2,
        attn_w_out_2, lru_w_in_2, lru_conv_w_2, lru_conv_b_2, lru_w_a_2, lru_b_a_2, lru_w_x_2,
        lru_b_x_2, lru_lambda_2, lru_w_out_2, final_g_2,
    )


_drawn_inputs = setup_inputs


def setup_inputs(seed=0):
    import zlib

    import numpy as np

    out = dict(_drawn_inputs(seed))
    spreads = {}
    factors = {'ffn_conv_b': 8.0,
     'mla_q_norm': 8.0,
     'mla_kv_norm': 8.0,
     'rel_bias_2': 8.0,
     'norm_g_2': 7.186,
     'ada_b_2': 3.603,
     'attn_sinks_2': 64.0,
     'attn_b_f_2': 4.105,
     'lru_conv_b_2': 6.17,
     'lru_w_a_2': 3.219,
     'lru_b_a_2': 64.0,
     'lru_b_x_2': 33.728}
    for name, (base, spread) in spreads.items():
        noise = np.random.default_rng([zlib.crc32(name.encode()), seed]).standard_normal(out[name].shape)
        drawn = base * np.exp(spread * noise) if base else spread * noise
        out[name] = __import__('jax').numpy.asarray(drawn.astype(out[name].dtype))
    for name, factor in factors.items():
        out[name] = (out[name] * factor).astype(out[name].dtype)
    return out
```

```python
from contextlib import ExitStack

import numpy as np

import concourse.bass as bass
from concourse import mybir

P = 128
D = 1024
KT = D // P
S = 256
QB = S // P
DFF = 2816
FT = DFF // P
FI = FT // 2
HEADS = 8
NOPE, ROPE, VD = 128, 64, 128
MLA_RANK = 256
HD2 = 64
CONV2 = 4
BUCKETS, EXACT, MAXDIST = 32, 16, 128
ALPHA = 4.0 ** 0.25
LN_EPS, RMS_EPS = 1e-5, 1e-6
NEG = -1e30
CAUSAL = P + S
LRU_C = 8.0
MAGIC = 1.5 * 2.0 ** 23
_a = np.float32(np.floor(2 * np.pi * 2 ** 8) / 2 ** 8)
_b = np.float32(np.floor((2 * np.pi - float(_a)) * 2 ** 19) / 2 ** 19)
TURN = [float(_a), float(_b), float(np.float32(2 * np.pi - float(_a) - float(_b)))]
PI_DOWN = float(np.nextafter(np.float32(np.pi), np.float32(0)))

ALU = mybir.AluOpType
ACT = mybir.ActivationFunctionType
AX = mybir.AxisListType
F32 = mybir.dt.float32
F32R = mybir.dt.float32r
I32 = mybir.dt.int32

RAW = 3
UNITS = 6
UL = 1024
AHEAD = UNITS - 1
MODRAW = 2
SD = 3

C_ID, C_SWAP32, C_SWAP64, C_DUP, C_DUPS = (i * P for i in range(5))
C_MASK = 5 * P
C_COL = C_MASK + CAUSAL
C_SELF, C_SEL1 = C_COL + 6, C_COL + 14
C_BUCKET = C_COL + 22
C_END = C_BUCKET + 2 * S

PB = [
    [("c", 8), ("c_2", 8), ("q_norm", 2), ("kv_norm", 2), ("norm_g", 16), ("final_g", 8), ("conv2_w", 32),
     ("conv2_b", 8), ("b_a", 8), ("b_x", 8), ("lam", 8)],
    [("mod_b", 96)],
    [("ada_b", 48), ("ln_g", 32), ("ln_b", 32)],
    [("conv_w0", 66), ("conv_b0", 22)],
    [("conv_w1", 66), ("conv_b1", 22)],
]


def constants():
    c = np.zeros((P, C_END), np.float32)
    i = np.arange(P)
    c[i, C_ID + i] = 1
    c[:, C_MASK:C_MASK + P] = np.where(i[None] <= i[:, None], 0, NEG)
    c[:, C_MASK + 2 * P:C_MASK + 3 * P] = c[:, C_MASK:C_MASK + P]
    c[i, C_SWAP32 + (i ^ 32)] = 1
    c[i, C_SWAP64 + (i ^ 64)] = 1
    j = np.arange(64)
    for h in range(2):
        c[j, C_DUP + 64 * h + j] = 1
        c[j, C_DUPS + 64 * h + (j ^ 32)] = 1
    c[:, C_COL] = (np.float32(10000.0) ** (-np.arange(32, dtype=np.float32) / 32))[i % 32]
    c[:, C_COL + 1] = np.where((i // 32) % 2 == 0, -1, 1)
    c[:, C_COL + 2] = i < 64
    c[:, C_COL + 3] = i >= 64
    dist = 255 - np.arange(2 * S)
    n = np.maximum(dist, 1)
    large = EXACT + (np.log(n / EXACT) / np.log(MAXDIST / EXACT) * (BUCKETS - EXACT)).astype(int)
    bucket = np.where(dist < EXACT, np.maximum(dist, 0), np.minimum(large, BUCKETS - 1))
    ok = (dist >= 0) & (dist < P)
    for b in range(BUCKETS):
        c[b, C_BUCKET:C_BUCKET + 2 * S] = (bucket == b) & ok
    c[BUCKETS, C_BUCKET:C_BUCKET + 2 * S] = ~ok
    root = HD2 ** 0.5
    c[0:8, C_COL + 4] = root
    c[8:16, C_COL + 5] = 1
    for h in range(8):
        c[8 + h, C_SELF + h] = -root
        c[h, C_SEL1 + h] = 1
    return c


def weight_stream(w):
    out = []

    def cols(key, src, n0, n=256, copies=1):
        out.append((key, [(src[:, n0:n0 + n].rearrange("(k p) c -> p k c", p=P), i * n) for i in range(copies)],
                    n * copies))

    def ffn(i):
        for it in range(FI + 1):
            if it < FI:
                cols(("ffa", i, it), w["ffn_w_in"][i], it * 256)
                cols(("ffb", i, it), w["ffn_w_in"][i], DFF + it * 256)
            if it:
                src = w["ffn_w_out"][i][(it - 1) * 256:it * 256, :]
                out.append((("ffo", i, it - 1), [(src.rearrange("(k p) c -> p k c", p=P), 0)], 1024))

    mla_in = w["mla_w_in"][0]
    cols(("mla_in", 0), mla_in, 0)
    cols(("mla_in", 1), mla_in, 256)
    cols(("mla_in", 2), mla_in, 512, 64)
    for j in range(2):
        for name, width in (("uq", 768), ("ukv", 1024)):
            src = w[f"mla_w_{name}"][0][:, j * width:(j + 1) * width]
            if name == "uq":
                src = src.rearrange("(k p) (h c) -> p k h c", p=P, h=4)
                out.append(((name, j), [(src[:, k:k + 1, :, a:b], at) for k in range(2)
                                        for a, b, at in ((0, NOPE, 0), (NOPE, NOPE + ROPE, 4 * NOPE))], width))
            else:
                out.append(((name, j), [(src.rearrange("(k p) c -> p k c", p=P), 0)], width))
    for m in range(4):
        cols(("mla_o", m), w["mla_w_o"][0], m * 256)
    ffn(0)
    for part in range(3):
        for m in range(4):
            cols(("moba_in", part * 4 + m), w["moba_w_in"][0], part * 1024 + m * 256)
    for m in range(4):
        cols(("moba_o", m), w["moba_w_o"][0], m * 256)
    ffn(1)
    ain = w["attn_w_in_2"][0]
    cols(("a_kv", 0), ain, 512)
    cols(("f", 0), ain, 2304, 8, 2)
    for m in range(2):
        cols(("a_q", m), ain, m * 256)
    for m in range(2):
        cols(("b_q", m), ain, 768 + m * 256)
    for m in range(2):
        cols(("b_k", m), ain, 1280 + m * 256)
    for m in range(2):
        cols(("b_v", m), ain, 1792 + m * 256)
    for m in range(4):
        cols(("a_gate", m), ain, 2312 + m * 256)
    for m in range(4):
        cols(("attn_o", m), w["attn_w_out_2"][0], m * 256)
    lin = w["lru_w_in_2"][0]
    for m in range(4):
        cols(("xr", m), lin, m * 256)
    for name in ("a", "x"):
        out.append(((f"w_{name}", 0), [(w[f"lru_w_{name}_2"][0].rearrange("n w v -> w n v"), 0)], 128))
    for m in range(4):
        cols(("l_gate", m), lin, 1024 + m * 256)
    for m in range(4):
        cols(("lru_o", m), w["lru_w_out_2"][0], m * 256)
    return out


def modulation_stream(w):
    mod, ada = w["mod_w"], w["ada_w_2"]
    out = []

    def rows(g, parts):
        for k in range(KT):
            out.append((g, k, [(src[k * P:(k + 1) * P, a:b], at) for src, a, b, at in parts]))

    groups = [
        [(mod[0], 0, 2048, 0)], [(mod[0], 2048, 4096, 0)], [(mod[0], 4096, 6144, 0)],
        [(mod[1], 0, 2048, 0)], [(mod[1], 2048, 4096, 0)], [(mod[1], 4096, 6144, 0)],
        [(ada[0], 0, 2048, 0)],
        [(ada[0], 2048, 3072, 0), (ada[1], 2048, 3072, 1024)],
        [(ada[1], 0, 2048, 0)],
    ]
    for g in (0, 1, 2):
        rows(g, groups[g])
    for pair in ((3, 4),):
        for k in range(KT):
            for g in pair:
                out.append((g, k, [(src[k * P:(k + 1) * P, a:b], at) for src, a, b, at in groups[g]]))
    for g in (5, 6):
        rows(g, groups[g])
    for k in range(KT):
        for g in (7, 8):
            out.append((g, k, [(src[k * P:(k + 1) * P, a:b], at) for src, a, b, at in groups[g]]))
    return out


def build(nc, w, consts, out):
    chunks = weight_stream(w)
    chunk_of = {key: n for n, (key, _, _) in enumerate(chunks)}
    row_tiles = [2 if key[0] in ("uq", "ukv", "ffo") else KT for key, _, _ in chunks]
    length = [k * width for k, (_, _, width) in zip(row_tiles, chunks)]
    mods = modulation_stream(w)
    NU = 2 * len(chunks)

    def unit0(*key):
        return 2 * chunk_of[key]

    landed, count = [], [0] * RAW
    for n, (_, parts, _) in enumerate(chunks):
        count[n % RAW] += 16 * len(parts)
        landed.append(count[n % RAW])
    mod_landed, count = [], [0] * MODRAW
    for n, (_, _, parts) in enumerate(mods):
        count[n % MODRAW] += 16 * len(parts)
        mod_landed.append(count[n % MODRAW])

    with ExitStack() as ctx:
        def sb(name, shape, dt=F32):
            return ctx.enter_context(nc.sbuf_tensor(name, shape, dt))

        sems = {}

        def sem(name):
            if name not in sems:
                sems[name] = ctx.enter_context(nc.semaphore(name))
            return sems[name]

        raw = sb("raw", [P, RAW, 2 * UL])
        modraw = sb("modraw", [P, MODRAW, 2048])
        w_hi = sb("w_hi", [P, UNITS, UL], F32R)
        w_lo = sb("w_lo", [P, UNITS, UL], F32R)
        h_hi = sb("h_hi", [P, KT * S], F32R)
        h_lo = sb("h_lo", [P, KT * S], F32R)
        o_hi = sb("o_hi", [P, KT * S], F32R)
        o_lo = sb("o_lo", [P, KT * S], F32R)
        x = sb("x", [P, KT * S])
        modsum = sb("modsum", [P, 2048])
        qz = sb("qz", [P, KT * S])
        kk = sb("kk", [P, 12 * S])
        vv = sb("vv", [P, 2 * 12 * P])
        of = sb("of", [P, KT * S])
        bias = sb("bias", [P, 8 * S])
        prob = sb("prob", [P, SD * CAUSAL])
        probT = sb("probT", [P, 2 * CAUSAL])
        cst = sb("cst", [P, C_BUCKET])
        cols = sb("cols", [P, 5 * P])
        modc = sb("modc", [P, 9 * 16])
        lncol = sb("lncol", [P, 12 * KT])
        gates = sb("gates", [P, 6 * KT])
        ones = sb("ones", [P, P])
        stat = sb("stat", [P, SD * 12])
        sinks = sb("sinks", [P, 8])
        small = sb("small", [P, 96])
        bf = sb("bf", [16, 1])
        rstd = sb("rstd", [P, 2 * S])
        relb = sb("relb", [BUCKETS + 1, 8])
        posq_i = sb("posq_i", [P, 2], I32)
        ebias = nc.dram_tensor("ebias", [8, P, CAUSAL], F32, kind="Internal").ap()
        bank = [ctx.enter_context(nc.psum_tensor(f"bank{i}", [P, 512], F32)) for i in range(8)]

        def tiles(t, a, b):
            return t[:, a * S:b * S]

        def grid(ap, n):
            return ap.rearrange("p (n s) -> p n s", n=n)

        def row_times(ap, n):
            return ap.rearrange("p (n s) -> p n s", n=1).broadcast_to([P, n, S])

        def head_cols(t, n):
            return t[:, n * CAUSAL:(n + 1) * CAUSAL]

        def const(at, n=1):
            return cst[:, at:at + n]

        def vtile(t, n, a=0, b=P):
            return vv[:, (t * 12 + n) * P + a:(t * 12 + n) * P + b]

        prow = kk[:, 0:5 * P]
        xrow = of[:, :]
        cos, sin, pos, angle = (tiles(bias, i, i + 1) for i in (0, 1, 6, 7))
        dist = bias[:, 2 * S:2 * S + CAUSAL]
        turns = bias[:, 4 * S:5 * S]
        pos_i = qz[:, 0:S].bitcast(I32)
        alibi = [vv[:, (t * 12 + 8) * P:(t * 12 + 8) * P + CAUSAL] for t in range(2)]
        mask = const(C_MASK, CAUSAL)
        ident = const(C_ID, P)
        half = [const(C_COL + 2), const(C_COL + 3)]
        hf = kk[:, 8 * S:12 * S]
        conv = kk[:, 8 * S:12 * S]
        gated = kk[:, 4 * S:8 * S]
        modacc = {g: modsum[:, :] for g in (0, 1, 2, 5, 6)}
        for a, b in ((3, 4), (7, 8)):
            modacc[a], modacc[b] = of[:, :], vv[:, 0:2048]
        pcol = {}
        for b, rows in enumerate(PB):
            at = b * P
            for name, n in rows:
                pcol[name] = cols[:, at:at + n]
                at += n
        c_act = small[:, 0:16]
        lam8 = small[:, 16:24]
        posq = small[:, 24:26]

        def unit_ap(ring, u):
            n = u // 2
            half_len = length[n] // 2
            return ring[:, (u % UNITS) * UL:(u % UNITS) * UL + half_len]

        w_hi_f, w_lo_f = w_hi[:, :, :].rearrange("p a b -> p (a b)"), w_lo[:, :, :].rearrange("p a b -> p (a b)")

        def hi(u):
            return unit_ap(w_hi_f, u)

        def lo(u):
            return unit_ap(w_lo_f, u)

        def raw_unit(u):
            n = u // 2
            half_len = length[n] // 2
            return raw[:, n % RAW, (u % 2) * half_len:(u % 2 + 1) * half_len]

        HEAD = {"mla": 0, "moba": 8, "swa": 16, "fgt": 24}
        SCALE = {"mla": (NOPE + ROPE) ** -0.5, "moba": 128 ** -0.5, "swa": HD2 ** -0.5, "fgt": HD2 ** -0.5}
        turn_keys = [("moba_in", i) for i in range(12)]
        turn_keys += [("a_kv", 0), ("f", 0)] + [(n, m) for n in ("a_q", "b_q", "b_k", "b_v") for m in range(2)]
        turn_keys += [("a_gate", m) for m in range(4)] + [("xr", m) for m in range(4)]
        turn_keys += [("l_gate", m) for m in range(4)]
        turn_of = {key: n for n, key in enumerate(turn_keys)}

        block = ctx.enter_context(nc.Block())

        @block.sync
        def _(sp):
            sp.dma_start(cst[:, :], consts[:, 0:C_BUCKET]).then_inc(sem("const_in"), 16)
            sp.dma_start(prob[0:BUCKETS + 1, 0:2 * S],
                         consts[0:BUCKETS + 1, C_BUCKET:C_END]).then_inc(sem("const_in"), 16)
            srcs = {
                "c": w["c"], "c_2": w["c_2"], "q_norm": w["mla_q_norm"], "kv_norm": w["mla_kv_norm"],
                "norm_g": w["norm_g_2"], "final_g": w["final_g_2"], "conv2_w": w["lru_conv_w_2"],
                "conv2_b": w["lru_conv_b_2"], "b_a": w["lru_b_a_2"], "b_x": w["lru_b_x_2"],
                "lam": w["lru_lambda_2"], "mod_b": w["mod_b"], "ada_b": w["ada_b_2"], "ln_g": w["ln_g"],
                "ln_b": w["ln_b"], "conv_w0": w["ffn_conv_w"][0], "conv_b0": w["ffn_conv_b"][0:1],
                "conv_w1": w["ffn_conv_w"][1], "conv_b1": w["ffn_conv_b"][1:2],
            }
            for b, rows in enumerate(PB):
                at = 0
                for name, n in rows:
                    s = srcs[name]
                    names = " ".join("abc"[:len(s.shape)])
                    if len(s.shape) > 1:
                        s = s.rearrange(f"{names} -> ({names})")
                    sp.dma_start(prow[at:at + n, b * P:(b + 1) * P],
                                 s.rearrange("(n q) -> n q", q=P)).then_inc(sem("params_in"), 16)
                    at += n
            sp.dma_start(xrow.rearrange("p (t f) -> p t f", t=2),
                         w["x"][0].rearrange("(t p) f -> p t f", p=P)).then_inc(sem("x_in"), 16)
            sp.dma_start(pos_i, w["positions"].broadcast_to([P, S])).then_inc(sem("pos_in"), 16)
            sp.dma_start(posq_i[:, :], w["positions"][0].rearrange("(t p) -> p t", p=P), allow_slow_non_contiguous=True).then_inc(sem("pos_in"), 16)
            sp.dma_start(sinks[:, :], w["attn_sinks_2"].broadcast_to([P, 8])).then_inc(sem("pos_in"), 16)
            for i in range(2):
                sp.dma_start(bf[8 * i:8 * i + 8, :], w["attn_b_f_2"].rearrange("a b -> b a"), allow_slow_non_contiguous=True).then_inc(
                    sem("pos_in"), 16)
            for n, (key, parts, width) in enumerate(chunks):
                if n >= RAW:
                    sp.wait_ge(sem("w_lo_ready"), 2 * (n - RAW) + 2)
                dst = raw[:, n % RAW, 0:length[n]].rearrange("p (k c) -> p k c", c=width)
                for i, (src, at) in enumerate(parts):
                    if key[0] == "uq":
                        to = dst[:, i // 2, at:at + 4 * src.shape[3]].rearrange("p (h c) -> p h c", h=4)
                        sp.dma_start(to, src[:, 0]).then_inc(sem(f"w_in{n % RAW}"), 16)
                    else:
                        sp.dma_start(dst[:, :, at:at + src.shape[2]], src).then_inc(sem(f"w_in{n % RAW}"), 16)
            for t in range(2):
                sp.wait_ge(sem("out_rows"), 2 * t + 2)
                sp.dma_start(out[0, t * P:(t + 1) * P, :], kk[:, t * D:(t + 1) * D]).then_inc(sem("stored"), 16)
            sp.wait_ge(sem("stored"), 32)

        N_PARAM = sum(len(rows) for rows in PB)

        @block.gpsimd
        def _(pool):
            pool.memset(ones[:, :], 1.0).then_inc(sem("ones"), 1)
            pool.dma_start(relb[0:BUCKETS, :], w["rel_bias_2"]).then_inc(sem("relb_in"), 16)

            def modulation(a, b):
                for n in range(a, b):
                    if n >= MODRAW:
                        pool.wait_ge(sem("mod_summed"), n - MODRAW + 1)
                    for src, at in mods[n][2]:
                        pool.dma_start(modraw[:, n % MODRAW, at:at + src.shape[1]], src).then_inc(
                            sem(f"mod_in{n % MODRAW}"), 16)

            modulation(0, KT)
            pool.wait_ge(sem("bias_row"), 1)
            pool.dma_start(ebias, probT[0:8, 0:CAUSAL].rearrange("h (q j) -> h q j", q=1).broadcast_to(
                [8, P, CAUSAL])).then_inc(sem("ebias_out"), 16)
            modulation(KT, 5 * KT)
            pool.wait_ge(sem("fold_summed"), 4 * 5)
            pool.wait_ge(sem("dist_ready"), 2)

            def alibi_table(h):
                if h >= 2:
                    pool.wait_ge(sem("shifted"), 8 + h - 1)
                pool.tensor_scalar(alibi[h % 2], dist, -(2.0 ** -(h + 1)) / SCALE["moba"], None,
                                   ALU.mult).then_inc(sem("alibi"), 1)

            alibi_table(0)
            alibi_table(1)
            modulation(5 * KT, 6 * KT + 2)
            for h in range(2, HEADS):
                alibi_table(h)
                modulation(6 * KT + h, 6 * KT + h + 1)
            modulation(7 * KT, len(mods))
            pool.wait_ge(sem("ebias_out"), 16)
            pool.wait_ge(sem("alibi"), 8)
            pool.wait_ge(sem("q_rotated"), 2)
            for h in range(8):
                src = bass.AP(ebias.tensor, h * P * CAUSAL + P - 1, [[CAUSAL - 1, P], [1, S]])
                pool.dma_start(tiles(bias, h, h + 1), src).then_inc(sem("bias_in"), 16)
            pool.wait_ge(sem("fold_summed"), 4 * 9)
            pool.memset(vv[:, :], 0.0).then_inc(sem("vv_zero"), 1)

        @block.tensor
        def _(pe):
            fold_n = [0]

            def start_unit(u):
                pe.wait_ge(sem("w_hi_ready"), u + 1)
                pe.wait_ge(sem("w_lo_ready"), u + 1)

            def feature_product(dst, u, cut, a_hi, a_lo, first, last):
                pe.matmul(dst, cut(hi(u)), a_hi, start=first, stop=False, skip_group_check=True)
                pe.matmul(dst, cut(hi(u)), a_lo, start=False, stop=False, skip_group_check=True)
                return pe.matmul(dst, cut(lo(u)), a_hi, start=False, stop=last, skip_group_check=True)

            def token_product(dst, u, cut, a_hi, a_lo, first, last):
                pe.matmul(dst, a_hi, cut(hi(u)), start=first, stop=False, skip_group_check=True)
                pe.matmul(dst, a_hi, cut(lo(u)), start=False, stop=False, skip_group_check=True)
                return pe.matmul(dst, a_lo, cut(hi(u)), start=False, stop=last, skip_group_check=True)

            def columns_chunk(key, dst, a, width=256, rows=None):
                u0 = unit0(*key)
                step = min(width, P)
                for u in (u0, u0 + 1):
                    start_unit(u)
                    for k in range(4):
                        kt = 4 * (u - u0) + k
                        for f in range(width // step):
                            at = k * width + f * step
                            ins = feature_product(dst[0:step, f * S:(f + 1) * S], u,
                                                  lambda r: r[:, at:at + step], tiles(a[0], kt, kt + 1),
                                                  tiles(a[1], kt, kt + 1), kt == 0 and f == 0, kt == KT - 1)
                    if u == u0:
                        ins.then_inc(sem("w_used"), 1)
                return ins

            def end_chunk(ins):
                ins.then_inc(sem("w_used"), 1)

            def turn(key):
                n = turn_of[key]
                if n >= 4:
                    pe.wait_ge(sem("turn_read"), n - 3)
                return bank[n % 4]

            def fold(g, b):
                pe.wait_ge(sem("mod_summed"), max(n for n, m in enumerate(mods) if m[0] == g) + 1)
                for part in range(4):
                    n = fold_n[0]
                    if n >= 2:
                        pe.wait_ge(sem("fold_summed"), n - 1)
                    for i in range(4):
                        at = (4 * part + i) * P
                        ins = pe.transpose(bank[b[n % 2]][:, i * P:(i + 1) * P], modacc[g][:, at:at + P], ident)
                    ins.then_inc(sem("fold_turned"), 1)
                    fold_n[0] += 1

            def norm_sums(n, centered=True, between=lambda: None):
                if centered:
                    for m in range(KT):
                        pe.wait_ge(sem("z_ready"), 8 * n + m + 1)
                        ins = pe.matmul(bank[3][:, 0:S], ones[:, :], tiles(qz, m, m + 1), start=m == 0, stop=m == 7)
                    ins.then_inc(sem("mean_done"), 1)
                between()
                for m in range(KT):
                    pe.wait_ge(sem("squared"), 8 * n + m + 1)
                    ins = pe.matmul(bank[2][:, 0:S], ones[:, :], tiles(kk, m, m + 1), start=m == 0, stop=m == 7)
                ins.then_inc(sem("var_done"), 1)

            def attention(kind, scores, value, pair):
                h0 = HEAD[kind]
                for t in range(HEADS + 3):
                    if t < HEADS:
                        g = h0 + t
                        if t >= 2:
                            pe.wait_ge(sem("shifted"), g - 1)
                        b = bank[t % 2]
                        ops = scores(t)
                        for i, (q, k) in enumerate(ops):
                            pe.matmul(b[:, 0:P], q[:, 0:P], k[:, 0:P], start=i == 0, stop=i == len(ops) - 1,
                                      skip_group_check=True)
                        for i, (q, k) in enumerate(ops):
                            ins = pe.matmul(b[:, P:CAUSAL], q[:, P:S], k[:, 0:S], start=False,
                                            stop=i == len(ops) - 1, skip_group_check=True)
                        ins.then_inc(sem("scores"), 1)
                    if 2 <= t < HEADS + 2:
                        g = h0 + t - 2
                        pe.wait_ge(sem("prob_ready"), g + 1)
                        if t >= 4:
                            pe.wait_ge(sem("probT_ready"), g - 1)
                        b = bank[2 + t % 2]
                        for i in range(3):
                            ins = pe.transpose(b[:, i * P:(i + 1) * P],
                                               prob[:, (g % SD) * CAUSAL + i * P:(g % SD) * CAUSAL + (i + 1) * P],
                                               ident)
                        ins.then_inc(sem("prob_turned"), 1)
                    if t >= 3:
                        h = t - 3
                        g = h0 + h
                        pe.wait_ge(sem("probT_ready"), g + 1)
                        n = (h // 2 if pair else h)
                        if n >= 2 and not (pair and h % 2):
                            pe.wait_ge(sem("pair_read" if pair else "o_ready"), outs0[kind] + n - 1)
                        dst = bank[(4, 7)[n % 2]][:, 0:S]
                        pt = head_cols(probT, g % 2)
                        first = not (pair and h % 2)
                        pe.matmul(dst, value(h, 0), pt[:, 0:S], start=first, stop=False, skip_group_check=True)
                        ins = pe.matmul(dst[:, P:S], value(h, 1), pt[:, S:CAUSAL], start=False, stop=True,
                                        skip_group_check=True)
                        ins.then_inc(sem("head_out"), 1)

            outs0 = {"mla": 0, "moba": 8, "swa": 0, "fgt": 4}

            residual = {"mla_o": 0, "moba_o": 2, "attn_o": 4, "lru_o": 5}

            def out_projection(name):
                for m in range(4):
                    if m >= 2:
                        pe.wait_ge(sem("z_ready"), 8 * residual[name] + 2 * (m - 1))
                    end_chunk(columns_chunk((name, m), bank[5 + m % 2], (o_hi, o_lo)))

            def ffn(l):
                for i in range(FI + 1):
                    n = l * FI + i
                    if i < FI:
                        if n:
                            pe.wait_ge(sem("ff_conv"), 2 * n)
                        end_chunk(columns_chunk(("ffa", l, i), bank[0], (h_hi, h_lo)))
                        if n:
                            pe.wait_ge(sem("ff_gated"), n)
                        end_chunk(columns_chunk(("ffb", l, i), bank[1], (h_hi, h_lo)))
                    if i:
                        u0 = unit0("ffo", l, i - 1)
                        pe.wait_ge(sem("ff_g_ready"), n)
                        for u in (u0, u0 + 1):
                            start_unit(u)
                            k = 2 * ((n - 1) % 2) + u - u0
                            for m in range(KT):
                                first = i == 1 and u == u0 and m % 2 == 0
                                ins = feature_product(bank[4 + m // 2][:, (m % 2) * S:(m % 2 + 1) * S], u,
                                                      lambda r: r[:, m * P:(m + 1) * P], tiles(o_hi, k, k + 1),
                                                      tiles(o_lo, k, k + 1), first, i == FI and u > u0)
                            ins.then_inc(sem("w_used"), 1)

            def wait_h(e):
                pe.wait_ge(sem("h_ready"), 8 * e + 8)

            pe.wait_ge(sem("const_in"), 32)
            pe.wait_ge(sem("ones"), 2)
            pe.wait_ge(sem("params_in"), 16 * N_PARAM)
            for b, rows in enumerate(PB):
                n = sum(r[1] for r in rows)
                ins = pe.transpose(bank[b // 4][:, (b % 4) * P:(b % 4) * P + n], prow[0:n, b * P:(b + 1) * P],
                                   cst[0:n, C_ID:C_ID + n])
            ins.then_inc(sem("params_turned"), 1)
            pe.wait_ge(sem("x_in"), 16)
            for m in range(KT):
                for t in range(2):
                    at = (m % 2) * S + t * P
                    ins = pe.transpose(bank[4 + m // 2][:, at:at + P], xrow[:, t * D + m * P:t * D + (m + 1) * P],
                                       ident)
                ins.then_inc(sem("x_turned"), 1)
            pe.wait_ge(sem("relb_in"), 16)
            pe.matmul(bank[3][0:8, :], relb[:, :], prob[0:BUCKETS + 1, 0:2 * S], start=True,
                      stop=True).then_inc(sem("bias_turned"), 1)
            pe.wait_ge(sem("cols_ready"), 5)
            fold(0, (2, 0))

            wait_h(0)
            for j in range(2):
                end_chunk(columns_chunk(("mla_in", j), bank[j], (h_hi, h_lo)))
            pe.wait_ge(sem("fold_summed"), 4)
            end_chunk(columns_chunk(("mla_in", 2), bank[2], (h_hi, h_lo), 64))
            pe.wait_ge(sem("bias_row"), 1)
            for j in range(2):
                pe.wait_ge(sem("c_squared"), j + 1)
                for m in range(2):
                    ins = pe.matmul(bank[3][:, j * S:(j + 1) * S], ones[:, :], tiles(kk, 2 * j + m, 2 * j + m + 1),
                                    start=m == 0, stop=m == 1)
                ins.then_inc(sem("c_summed"), 1)
            pe.wait_ge(sem("kr_copied"), 1)
            pe.wait_ge(sem("x_copied"), 4)
            for i, at in enumerate((C_DUP, C_DUPS)):
                ins = pe.matmul(bank[4][:, i * S:(i + 1) * S], cst[0:64, at:at + P], tiles(kk, 4, 5)[0:64, :],
                                start=True, stop=True)
            ins.then_inc(sem("kr_spread"), 1)
            for j in range(2):
                u0 = unit0("uq", j)
                pe.wait_ge(sem("c_ready"), 2)
                if j:
                    pe.wait_ge(sem("uq_copied"), 3)
                for u in (u0, u0 + 1):
                    start_unit(u)
                    kt = u - u0
                    a = tiles(o_hi, kt, kt + 1), tiles(o_lo, kt, kt + 1)
                    for h in range(4):
                        feature_product(bank[5 + h // 2][:, (h % 2) * S:(h % 2 + 1) * S], u,
                                        lambda r: r[:, h * P:(h + 1) * P], *a, kt == 0 and h % 2 == 0, kt == 1)
                    for r2 in range(2):
                        ins = feature_product(
                            bank[7][:, r2 * S:(r2 + 1) * S], u,
                            lambda r: r[:, (4 + r2) * P:(5 + r2) * P],
                            *a, kt == 0 and r2 == 0, kt == 1)
                    if kt == 0:
                        ins.then_inc(sem("w_used"), 1)
                end_chunk(ins)
                pe.wait_ge(sem("uq_copied"), 3 * j + 3)
                pe.wait_ge(sem("c_rooted"), 2)
                if j:
                    pe.wait_ge(sem("q_rotated"), 1)
                for i in range(2):
                    ins = pe.matmul(bank[3][:, i * S:(i + 1) * S], const(C_SWAP32, P), tiles(of, 4 + i, 5 + i),
                                    start=True, stop=True)
                ins.then_inc(sem("q_swapped"), 1)
                u0 = unit0("ukv", j)
                pe.wait_ge(sem("kr_ready"), 1)
                if j:
                    pe.wait_ge(sem("ukv_copied"), 4)
                for u in (u0, u0 + 1):
                    start_unit(u)
                    kt = u - u0
                    a = tiles(o_hi, 2 + kt, 3 + kt), tiles(o_lo, 2 + kt, 3 + kt)
                    for h in range(4):
                        feature_product(bank[h // 2][:, (h % 2) * S:(h % 2 + 1) * S], u,
                                        lambda r: r[:, h * 256:h * 256 + P], *a, kt == 0 and h % 2 == 0, kt == 1)
                    for t in range(2):
                        ins = token_product(
                            bank[2 + 2 * t][:, :], u,
                            lambda r: r.rearrange("p (h c) -> p h c", h=4)[:, :, NOPE:256],
                            a[0][:, t * P:(t + 1) * P], a[1][:, t * P:(t + 1) * P], kt == 0, kt == 1)
                    if kt == 0:
                        ins.then_inc(sem("w_used"), 1)
                end_chunk(ins)
            pe.wait_ge(sem("uq_copied"), 6)
            fold(1, (5, 6))
            pe.wait_ge(sem("ukv_copied"), 8)
            pe.wait_ge(sem("q_rotated"), 2)
            attention("mla",
                      lambda h: [(tiles(qz, h, h + 1), tiles(kk, h, h + 1)),
                                 (tiles(of, h // 2, h // 2 + 1), tiles(of, 6 + h % 2, 7 + h % 2))],
                      lambda h, t: vtile(t, h), False)
            pe.wait_ge(sem("shifted"), 8)
            fold(2, (0, 1))
            pe.wait_ge(sem("o_ready"), 8)
            out_projection("mla_o")
            norm_sums(0)
            wait_h(1)
            ffn(0)
            norm_sums(1, between=lambda: fold(3, (0, 1)))
            wait_h(2)

            for i in range(8):
                end_chunk(columns_chunk(("moba_in", i), turn(("moba_in", i)), (h_hi, h_lo)))
                if i == 1:
                    fold(4, (5, 6))

            def token_chunk(key):
                b = turn(key)
                u0 = unit0(*key)
                for u in (u0, u0 + 1):
                    start_unit(u)
                    for k in range(4):
                        kt = 4 * (u - u0) + k
                        for t in range(2):
                            at = kt * S + t * P
                            ins = token_product(b[:, t * S:(t + 1) * S], u, lambda r: r[:, k * 256:(k + 1) * 256],
                                                h_hi[:, at:at + P], h_lo[:, at:at + P], kt == 0 and t == 0,
                                                kt == KT - 1)
                    if u == u0:
                        ins.then_inc(sem("w_used"), 1)
                end_chunk(ins)

            for i in range(8, 12):
                token_chunk(("moba_in", i))
            pe.wait_ge(sem("turn_read"), 12)
            fold(5, (5, 6))
            attention("moba", lambda h: [(tiles(qz, h, h + 1), tiles(kk, h, h + 1))],
                      lambda h, t: vtile(t, h), False)
            pe.wait_ge(sem("shifted"), 16)
            fold(6, (0, 1))
            pe.wait_ge(sem("o_ready"), 16)
            out_projection("moba_o")
            norm_sums(2)
            wait_h(3)
            ffn(1)
            norm_sums(3)
            norm_sums(4, False)

            wait_h(4)
            key = ("a_kv", 0)
            end_chunk(columns_chunk(key, turn(key), (h_hi, h_lo)))
            key = ("f", 0)
            end_chunk(columns_chunk(key, turn(key), (h_hi, h_lo), 16))
            for name in ("a_q", "b_q"):
                for m in range(2):
                    end_chunk(columns_chunk((name, m), turn((name, m)), (h_hi, h_lo)))
                fold(7 if name == "a_q" else 8, (5, 6))
            pe.wait_ge(sem("turn_read"), turn_of[("a_kv", 0)] + 1)
            pe.matmul(bank[4][:, 0:S], const(C_SWAP64, P), tiles(kk, 8, 9), start=True, stop=True)
            for t in range(2):
                ins = pe.transpose(bank[4][:, S + t * P:S + (t + 1) * P], tiles(kk, 9, 10)[:, t * P:(t + 1) * P],
                                   ident)
            ins.then_inc(sem("akv_turned"), 1)
            for m in range(2):
                end_chunk(columns_chunk(("b_k", m), turn(("b_k", m)), (h_hi, h_lo)))
            for m in range(2):
                token_chunk(("b_v", m))
            pe.wait_ge(sem("turn_read"), turn_of[("b_v", 1)] + 1)
            pe.wait_ge(sem("akv_spread"), 8)
            attention("swa",
                      lambda h: [(tiles(qz, h // 2, h // 2 + 1), tiles(kk, h // 4 * 2 + h % 2, h // 4 * 2 + h % 2 + 1))],
                      lambda h, t: vtile(t, h // 4 * 2 + h % 2), True)
            pe.wait_ge(sem("decay_ready"), 9)
            pe.wait_ge(sem("shifted"), 24)
            pe.wait_ge(sem("probT_ready"), 24)
            pe.wait_ge(sem("pair_read"), 4)
            attention("fgt",
                      lambda h: [(tiles(qz, 4 + h // 2, 5 + h // 2), tiles(kk, 4 + h, 5 + h)),
                                 (rstd[:, S:2 * S], tiles(bias, h, h + 1))],
                      lambda h, t: vtile(t, 4 + h), True)
            pe.wait_ge(sem("shifted"), 32)
            for m in range(4):
                key = ("a_gate", m)
                end_chunk(columns_chunk(key, turn(key), (h_hi, h_lo)))
            pe.wait_ge(sem("o_ready"), 20)
            out_projection("attn_o")
            norm_sums(5, False)

            wait_h(5)
            for m in range(4):
                key = ("xr", m)
                end_chunk(columns_chunk(key, turn(key), (h_hi, h_lo)))
            pe.wait_ge(sem("turn_read"), turn_of[("xr", 3)] + 1)
            pe.wait_ge(sem("z_ready"), 40)
            for i, name in enumerate(("w_a", "w_x")):
                u0 = unit0(name, 0)
                for u in (u0, u0 + 1):
                    start_unit(u)
                    for k in range(4):
                        n = 4 * (u - u0) + k
                        if i == 0:
                            pe.wait_ge(sem("xc_ready"), n // 2 + 1)
                        ins = feature_product(bank[4 * i + n // 2][:, (n % 2) * S:(n % 2 + 1) * S], u,
                                              lambda r: r[:, k * P:(k + 1) * P], tiles(o_hi, n, n + 1),
                                              tiles(o_lo, n, n + 1), True, True)
                    ins.then_inc(sem("w_used"), 1)
            pe.wait_ge(sem("rg_read"), 8)
            for m in range(4):
                key = ("l_gate", m)
                end_chunk(columns_chunk(key, turn(key), (h_hi, h_lo)))
            pe.wait_ge(sem("rg_read"), 16)
            pe.wait_ge(sem("o_ready"), 24)
            out_projection("lru_o")
            norm_sums(6, False)
            for t in range(2):
                for m in range(KT):
                    pe.wait_ge(sem("h_full"), 8 * 6 + m + 1)
                    b = bank[4 + 2 * t + m // 4]
                    ins = pe.transpose(b[:, (m % 4) * P:(m % 4 + 1) * P], qz[:, m * S + t * P:m * S + (t + 1) * P],
                                       ident)
                    if m % 4 == 3:
                        ins.then_inc(sem("y_turned"), 1)

        @block.scalar
        def _(act):
            nxt = [0]

            def ahead(u):
                while nxt[0] <= min(u, NU - 1):
                    v = nxt[0]
                    if v % 2 == 0:
                        act.wait_ge(sem(f"w_in{v // 2 % RAW}"), landed[v // 2])
                    if v >= UNITS:
                        act.wait_ge(sem("w_used"), v - UNITS + 1)
                    act.activation(hi(v), raw_unit(v), ACT.Copy).then_inc(sem("w_hi_ready"), 1)
                    nxt[0] += 1

            def product(*key):
                u = unit0(*key) + 1
                ahead(u + AHEAD)
                act.wait_ge(sem("w_used"), u + 1)

            def h_high(e, m):
                act.wait_ge(sem("h_full"), 8 * e + m + 1)
                act.activation(tiles(h_hi, m, m + 1), tiles(hf, m % 4, m % 4 + 1), ACT.Copy).then_inc(
                    sem("h_hi_ready"), 1)

            def norm(n, e, eps):
                for m in range(KT):
                    if n < 4:
                        act.wait_ge(sem("centered"), 8 * n + m + 1)
                    elif n == 4:
                        act.wait_ge(sem("x_ready"), 24 + m + 1)
                    else:
                        act.wait_ge(sem("z_ready"), 8 * (n - 1) + m + 1)
                    act.activation(tiles(kk, m, m + 1), tiles(qz if n < 4 else x, m, m + 1),
                                   ACT.Square).then_inc(sem("squared"), 1)
                act.wait_ge(sem("var_done"), n + 1)
                act.activation(rstd[:, 0:S], bank[2][:, 0:S], ACT.Sqrt, bias=eps, scale=1.0 / D).then_inc(
                    sem("rooted"), 1)
                if e is None and n != 3:
                    return
                for m in range(KT):
                    if e is not None:
                        h_high(e, m)
                    if n < 4:
                        act.wait_ge(sem("normed"), 8 * n + m + 1)
                        act.activation(tiles(x, m, m + 1), tiles(qz, m, m + 1), ACT.Identity,
                                       bias=pcol["ln_b"][:, 8 * n + m:8 * n + m + 1],
                                       scale=pcol["ln_g"][:, 8 * n + m:8 * n + m + 1]).then_inc(sem("x_ready"), 1)

            def attention(kind, pair, first_unit):
                h0 = HEAD[kind]
                sc = SCALE[kind]
                ahead(first_unit + AHEAD)
                for t in range(HEADS + 3):
                    if t < HEADS:
                        g = h0 + t
                        p = head_cols(prob, g % SD)
                        st = stat[:, (g % SD) * 12:(g % SD + 1) * 12]
                        act.wait_ge(sem("shifted"), g + 1)
                        act.activation(p[:, 0:P], p[:, 0:P], ACT.Exp, bias=st[:, 2:3], scale=sc,
                                       accum_out=st[:, 4:5]).then_inc(sem("exped"), 1)
                        act.activation(p[:, P:CAUSAL], p[:, P:CAUSAL], ACT.Exp, bias=st[:, 3:4], scale=sc,
                                       accum_out=st[:, 5:6]).then_inc(sem("exped"), 1)
                        if kind == "swa":
                            act.activation(st[:, 8:10], st[:, 2:4], ACT.Exp,
                                           bias=sinks[:, t:t + 1]).then_inc(sem("sink_ready"), 1)
                    if 2 <= t < HEADS + 2:
                        g = h0 + t - 2
                        act.wait_ge(sem("prob_turned"), g + 1)
                        if g >= 2:
                            act.wait_ge(sem("head_out"), g - 1)
                        elif g == 0:
                            act.wait_ge(sem("ebias_out"), 16)
                        act.activation(head_cols(probT, g % 2), bank[2 + t % 2][:, 0:CAUSAL],
                                       ACT.Copy).then_inc(sem("probT_ready"), 1)
                    if t >= 3:
                        h = t - 3
                        if not pair:
                            act.wait_ge(sem("head_out"), h0 + h + 1)
                            act.activation(tiles(o_hi, h, h + 1), bank[(4, 7)[h % 2]][:, 0:S],
                                           ACT.Copy).then_inc(sem("o_hi_ready"), 1)
                        elif h % 2:
                            act.wait_ge(sem("head_out"), h0 + h + 1)
                            n = h // 2 + (4 if kind == "fgt" else 0)
                            act.activation(tiles(of, n, n + 1), bank[(4, 7)[h // 2 % 2]][:, 0:S],
                                           ACT.Copy).then_inc(sem("pair_read"), 1)

            def ffn(l):
                w2, cb = pcol[f"conv_w{l}"], pcol[f"conv_b{l}"]
                for i in range(FI):
                    n = l * FI + i
                    product("ffa", l, i)
                    for t in range(2):
                        f = 2 * i + t
                        s = 2 * (n % 2) + t
                        act.activation(tiles(conv, s, s + 1), bank[0][:, t * S:(t + 1) * S], ACT.Identity,
                                       bias=cb[:, f:f + 1], scale=w2[:, 2 * FT + f:2 * FT + f + 1]).then_inc(
                                           sem("ff_c0"), 1)
                    s = 2 * (n % 2)
                    act.wait_ge(sem("ff_conv"), 2 * n + 2)
                    act.activation(tiles(gated, s, s + 2), tiles(conv, s, s + 2), ACT.Gelu_apprx_tanh).then_inc(
                        sem("ff_gelu"), 1)
                    product("ffb", l, i)
                    act.wait_ge(sem("ff_gated"), n + 1)
                    act.activation(tiles(o_hi, s, s + 2), tiles(gated, s, s + 2), ACT.Copy).then_inc(
                        sem("ff_g_hi"), 1)
                product("ffo", l, FI - 1)

            act.wait_ge(sem("params_turned"), 1)
            for b, rows in enumerate(PB):
                n = sum(r[1] for r in rows)
                act.activation(cols[:, b * P:b * P + n], bank[b // 4][:, (b % 4) * P:(b % 4) * P + n],
                               ACT.Copy).then_inc(sem("cols_ready"), 1)
            act.wait_ge(sem("cols_ready"), 1)
            act.activation(c_act, cols[:, 0:16], ACT.Silu).then_inc(sem("c_act"), 1)
            for m in range(4):
                act.wait_ge(sem("x_turned"), 2 * m + 2)
                act.activation(tiles(x, 2 * m, 2 * m + 2), bank[4 + m][:, :], ACT.Copy).then_inc(sem("x_copied"), 1)
            act.wait_ge(sem("bias_turned"), 1)
            act.activation(probT[0:8, 0:2 * S], bank[3][0:8, :], ACT.Copy, scale=1 / SCALE["swa"]).then_inc(
                sem("bias_row"), 1)
            ahead(AHEAD)
            act.wait_ge(sem("turned_angles"), 2)
            act.activation(cos, cos, ACT.Sin).then_inc(sem("rotary"), 1)
            act.activation(sin, sin, ACT.Sin, scale=const(C_COL + 1)).then_inc(sem("rotary"), 1)
            for m in range(KT):
                h_high(0, m)

            for j in range(2):
                product("mla_in", j)
                act.activation(tiles(kk, 2 * j, 2 * j + 2), bank[j][:, :], ACT.Square).then_inc(sem("c_squared"), 1)
            product("mla_in", 2)
            act.activation(tiles(kk, 4, 5)[0:64, :], bank[2][0:64, 0:S], ACT.Copy).then_inc(sem("kr_copied"), 1)
            act.wait_ge(sem("c_summed"), 2)
            for j in range(2):
                act.activation(tiles(rstd, j, j + 1), bank[3][:, j * S:(j + 1) * S], ACT.Sqrt, bias=RMS_EPS,
                               scale=1.0 / MLA_RANK).then_inc(sem("c_rooted"), 1)
            for j in range(2):
                act.wait_ge(sem("c_full"), 2 * j + 2)
                act.activation(tiles(o_hi, 2 * j, 2 * j + 2), tiles(hf, 2 * j, 2 * j + 2), ACT.Copy).then_inc(
                    sem("c_hi"), 1)
            for j in range(2):
                product("uq", j)
                act.activation(tiles(qz, 4 * j, 4 * j + 2), bank[5][:, :], ACT.Copy).then_inc(sem("uq_copied"), 1)
                act.activation(tiles(qz, 4 * j + 2, 4 * j + 4), bank[6][:, :], ACT.Copy).then_inc(sem("uq_copied"), 1)
                if j:
                    act.wait_ge(sem("q_rotated"), 1)
                act.activation(tiles(of, 4, 6), bank[7][:, :], ACT.Copy).then_inc(sem("uq_copied"), 1)
                product("ukv", j)
                if j:
                    act.wait_ge(sem("kr_ready"), 1)
                for i in range(2):
                    act.activation(tiles(kk, 4 * j + 2 * i, 4 * j + 2 * i + 2), bank[i][:, :], ACT.Copy).then_inc(
                        sem("ukv_copied"), 1)
                for t in range(2):
                    at = (t * 12 + 4 * j) * P
                    act.activation(vv[:, at:at + 4 * P], bank[2 + 2 * t][:, :], ACT.Copy).then_inc(
                        sem("ukv_copied"), 1)
            attention("mla", False, unit0("mla_o", 0))
            for m in range(4):
                product("mla_o", m)
            norm(0, 1, LN_EPS / ALPHA ** 2)
            ffn(0)
            norm(1, 2, LN_EPS / ALPHA ** 2)

            def turned(key):
                product(*key)
                return bank[turn_of[key] % 4]

            for i in range(8):
                b = turned(("moba_in", i))
                dst = qz if i < 4 else kk
                act.activation(tiles(dst, 2 * (i % 4), 2 * (i % 4) + 2), b[:, :], ACT.Copy).then_inc(
                    sem("turn_read"), 1)
            for i in range(4):
                b = turned(("moba_in", 8 + i))
                dst = vv[:, :].rearrange("p (t f) -> p t f", t=2)[:, :, 2 * i * P:(2 * i + 2) * P]
                act.activation(dst, grid(b[:, :], 2), ACT.Copy).then_inc(sem("turn_read"), 1)
            attention("moba", False, unit0("moba_o", 0))
            for m in range(4):
                product("moba_o", m)
            norm(2, 3, LN_EPS / ALPHA ** 2)
            ffn(1)
            norm(3, None, LN_EPS / ALPHA ** 2)
            norm(4, 4, RMS_EPS)

            b = turned(("a_kv", 0))
            act.activation(tiles(kk, 8, 10), b[:, :], ACT.Copy).then_inc(sem("turn_read"), 1)
            b = turned(("f", 0))
            act.activation(prob[0:16, 0:S], b[0:16, 0:S], ACT.Identity, bias=bf[:, :]).then_inc(sem("turn_read"), 1)
            for i, name in enumerate(("a_q", "b_q")):
                for m in range(2):
                    b = turned((name, m))
                    at = 4 * i + 2 * m
                    act.activation(tiles(qz, at, at + 2), b[:, :], ACT.Copy).then_inc(sem("turn_read"), 1)
            act.wait_ge(sem("f_abs"), 1)
            act.activation(prob[0:16, 2 * S:3 * S], prob[0:16, S:2 * S], ACT.Exp, scale=-1.0).then_inc(
                sem("f_exp"), 1)
            act.wait_ge(sem("akv_turned"), 1)
            act.wait_ge(sem("akv_spread"), 8)
            for m in range(2):
                b = turned(("b_k", m))
                dst = grid(kk[:, (4 + 4 * m) * S:(8 + 4 * m) * S], 2)
                act.activation(dst[:, :, 0:S], grid(b[:, :], 2), ACT.Copy, scale=half[0]).then_inc(
                    sem("bk_low"), 1)
                act.activation(dst[:, :, S:2 * S], grid(b[:, :], 2), ACT.Copy, scale=half[1]).then_inc(
                    sem("turn_read"), 1)
            act.wait_ge(sem("vv_zero"), 1)
            for m in range(2):
                b = turned(("b_v", m))
                for o in range(2):
                    src = b[:, :].rearrange("p (t i o f) -> p t i o f", t=2, i=2, o=2)[:, :, :, o, :]
                    dst = vv[:, :].rearrange("p (t i o f) -> p t i o f", t=2, i=6, o=2)
                    dst = dst[:, :, 2 + 2 * m:4 + 2 * m, o, o * 64:(o + 1) * 64]
                    for t in range(2):
                        last = act.activation(dst[:, t], src[:, t], ACT.Copy)
                        last.then_inc(sem("turn_read" if o and t else "bv_part"), 1)
            attention("swa", True, unit0("a_gate", 0))
            attention("fgt", True, unit0("a_gate", 0))
            for m in range(4):
                b = turned(("a_gate", m))
                if m >= 2:
                    act.wait_ge(sem("head_gated"), m - 1)
                act.activation(prob[:, (m % 2) * 512:(m % 2 + 1) * 512], b[:, :], ACT.Silu).then_inc(
                    sem("turn_read"), 1)
                act.wait_ge(sem("head_gated"), m + 1)
                act.activation(tiles(o_hi, 2 * m, 2 * m + 2), tiles(of, 2 * m, 2 * m + 2), ACT.Copy).then_inc(
                    sem("o_hi_ready"), 1)
            for m in range(4):
                product("attn_o", m)
            norm(5, 5, RMS_EPS)

            act.wait_ge(sem("lam_abs"), 1)
            act.activation(small[:, 48:56], small[:, 40:48], ACT.Exp, scale=-1.0).then_inc(
                sem("lam_exp"), 1)
            for m in range(4):
                b = turned(("xr", m))
                for t in range(2):
                    f = 2 * m + t
                    act.activation(tiles(kk, f, f + 1), b[:, t * S:(t + 1) * S], ACT.Identity,
                                   bias=pcol["conv2_b"][:, f:f + 1],
                                   scale=pcol["conv2_w"][:, 24 + f:25 + f]).then_inc(sem("xc_started"), 1)
                act.wait_ge(sem("xc_full"), 2 * m + 2)
                act.activation(tiles(o_hi, 2 * m, 2 * m + 2), tiles(kk, 2 * m, 2 * m + 2), ACT.Copy).then_inc(
                    sem("xc_hi"), 1)
            for i, (name, dst, pb) in enumerate((("w_a", qz, "b_a"), ("w_x", vv, "b_x"))):
                product(name, 0)
                for n in range(KT):
                    act.activation(tiles(dst, n, n + 1), bank[4 * i + n // 2][:, (n % 2) * S:(n % 2 + 1) * S],
                                   ACT.Sigmoid, bias=pcol[pb][:, n:n + 1]).then_inc(sem("rg_read"), 1)
            ahead(unit0("l_gate", 0) + AHEAD)
            for i in range(2):
                act.wait_ge(sem("rate_ready"), 4 * i + 4)
                act.activation(tiles(bias, 4 * i, 4 * i + 4), tiles(qz, 4 * i, 4 * i + 4), ACT.Tanh).then_inc(
                    sem("rate_tanh"), 1)
                act.wait_ge(sem("rate_tanh"), i + 1)
                act.activation(tiles(qz, 4 * i, 4 * i + 4), tiles(qz, 4 * i, 4 * i + 4), ACT.Exp).then_inc(
                    sem("decay_exp"), 1)
            ahead(unit0("l_gate", 0) + 1 + AHEAD)
            for i in range(2):
                act.wait_ge(sem("ratio_ready"), i + 1)
                act.activation(tiles(of, 4 * i, 4 * i + 4), tiles(of, 4 * i, 4 * i + 4), ACT.Sqrt,
                               scale=-2.0).then_inc(sem("input_root"), 1)
            for m in range(4):
                b = turned(("l_gate", m))
                act.wait_ge(sem("ix_ready"), m // 2 + 1)
                act.activation(tiles(kk, 2 * m, 2 * m + 2), b[:, :], ACT.Silu).then_inc(sem("turn_read"), 1)
                act.wait_ge(sem("l_gated"), m + 1)
                act.activation(tiles(o_hi, 2 * m, 2 * m + 2), tiles(kk, 2 * m, 2 * m + 2), ACT.Copy).then_inc(
                    sem("o_hi_ready"), 1)
            for m in range(4):
                product("lru_o", m)
            norm(6, None, RMS_EPS)
            for t in range(2):
                for i in range(2):
                    act.wait_ge(sem("y_turned"), 2 * t + i + 1)
                    at = t * D + i * 512
                    act.activation(kk[:, at:at + 512], bank[4 + 2 * t + i][:, :], ACT.Copy).then_inc(
                        sem("out_rows"), 1)

        @block.vector
        def _(dve):
            nxt, mod_n, fold_n, chain = [0], [0], [0], [0]

            def link(ins):
                chain[0] += 1
                ins.then_inc(sem("vec_step"), 1)
                dve.wait_ge(sem("vec_step"), chain[0])

            def magnitude(dst, src):
                return dve.scalar_tensor_tensor(dst, src, -1.0, src, ALU.mult, ALU.max)

            def ahead(u):
                while nxt[0] <= min(u, NU - 1):
                    v = nxt[0]
                    dve.wait_ge(sem("w_hi_ready"), v + 1)
                    dve.tensor_tensor(lo(v), raw_unit(v), hi(v).bitcast(F32), ALU.subtract).then_inc(
                        sem("w_lo_ready"), 1)
                    nxt[0] += 1

            def product(*key):
                u = unit0(*key) + 1
                ahead(u + AHEAD)
                dve.wait_ge(sem("w_used"), u + 1)

            def modulate(count):
                for n in range(mod_n[0], mod_n[0] + count):
                    g, k, _ = mods[n]
                    acc = modacc[g]
                    ck = c_act[:, (8 if g >= 6 else 0) + k:(8 if g >= 6 else 0) + k + 1]
                    src = modraw[:, n % MODRAW, :]
                    dve.wait_ge(sem(f"mod_in{n % MODRAW}"), mod_landed[n])
                    if k == 0:
                        if g in (1, 2, 5, 6):
                            dve.wait_ge(sem("fold_turned"), 4 * (3 if g == 5 else g))
                        ins = dve.tensor_scalar(acc, src, ck, None, ALU.mult)
                    else:
                        dve.wait_ge(sem("mod_summed"), n)
                        ins = dve.scalar_tensor_tensor(acc, src, ck, acc, ALU.mult, ALU.add)
                    ins.then_inc(sem("mod_summed"), 1)
                mod_n[0] += count

            def fold(g, b):
                for part in range(4):
                    n = fold_n[0]
                    dve.wait_ge(sem("fold_turned"), n + 1)
                    at = 16 * g + 4 * part
                    dve.tensor_reduce(modc[:, at:at + 4],
                                      bank[b[n % 2]][:, :].rearrange("p (i c) -> p i c", i=4),
                                      AX.X, ALU.add).then_inc(sem("fold_summed"), 1)
                    fold_n[0] += 1
                dve.wait_ge(sem("fold_summed"), fold_n[0])
                biases = {6: [("ada_b", 0, 16)], 7: [("ada_b", 16, 8), ("ada_b", 40, 8)], 8: [("ada_b", 24, 16)]}
                at = 16 * g
                for name, r, n in biases.get(g, [("mod_b", 16 * g, 16)]):
                    link(dve.tensor_tensor(modc[:, at:at + n], modc[:, at:at + n], pcol[name][:, r:r + n],
                                           ALU.add))
                    at += n

            def mod8(g, half):
                return modc[:, 16 * g + 8 * half:16 * g + 8 * half + 8]

            def coefficients(e, shift, scale, gain=None, offset=None):
                cs, ct = lncol[:, 16 * e:16 * e + 8], lncol[:, 16 * e + 8:16 * e + 16]
                link(dve.tensor_scalar(cs, scale, 1.0, None, ALU.add))
                if offset is not None:
                    link(dve.tensor_tensor(ct, offset, cs, ALU.mult))
                    link(dve.tensor_tensor(ct, ct, shift, ALU.add))
                else:
                    link(dve.tensor_copy(ct, shift))
                if gain is not None:
                    link(dve.tensor_tensor(cs, cs, gain, ALU.mult))

            def gate(r, src, scale):
                link(dve.tensor_scalar(gates[:, 8 * r:8 * r + 8], src, scale, None, ALU.mult))

            def h_full(e, m, src):
                dve.tensor_scalar(tiles(hf, m % 4, m % 4 + 1), src, lncol[:, 16 * e + m:16 * e + m + 1],
                                  lncol[:, 16 * e + 8 + m:16 * e + 9 + m], ALU.mult, ALU.add).then_inc(
                                      sem("h_full"), 1)

            def h_low(e, m):
                dve.wait_ge(sem("h_hi_ready"), 8 * e + m + 1)
                dve.tensor_tensor(tiles(h_lo, m, m + 1), tiles(hf, m % 4, m % 4 + 1),
                                  tiles(h_hi, m, m + 1).bitcast(F32), ALU.subtract).then_inc(sem("h_ready"), 1)

            def residual(r, m, y):
                dve.scalar_tensor_tensor(tiles(qz if r < 4 else x, m, m + 1), y, gates[:, 8 * r + m:8 * r + m + 1],
                                         tiles(x, m, m + 1), ALU.mult, ALU.add).then_inc(sem("z_ready"), 1)

            def out_projection(name, r):
                for i in range(4):
                    product(name, i)
                    for t in range(2):
                        residual(r, 2 * i + t, bank[5 + i % 2][:, t * S:(t + 1) * S])

            def norm(n, e, between=lambda: None):
                if n < 4:
                    dve.wait_ge(sem("mean_done"), n + 1)
                    for m in range(KT):
                        dve.scalar_tensor_tensor(tiles(qz, m, m + 1), bank[3][:, 0:S], -1.0 / D,
                                                 tiles(qz, m, m + 1), ALU.mult, ALU.add).then_inc(
                                                     sem("centered"), 1)
                between()
                dve.wait_ge(sem("rooted"), n + 1)
                link(dve.reciprocal(tiles(rstd, 1, 2), tiles(rstd, 0, 1)))
                for m in range(KT + 2):
                    if m < KT:
                        dve.tensor_tensor(tiles(qz, m, m + 1), tiles(qz if n < 4 else x, m, m + 1),
                                          tiles(rstd, 1, 2), ALU.mult).then_inc(sem("normed"), 1)
                    if 1 <= m <= KT and (e is not None or n == 6):
                        dve.wait_ge(sem("normed"), 8 * n + m)
                        if n == 6:
                            f = pcol["final_g"][:, m - 1:m]
                            dve.tensor_scalar(tiles(qz, m - 1, m), tiles(qz, m - 1, m), f, None,
                                              ALU.mult).then_inc(sem("h_full"), 1)
                        else:
                            h_full(e, m - 1, tiles(qz, m - 1, m))
                    if m >= 2 and e is not None:
                        h_low(e, m - 2)

            def attention(kind, pair, first_unit, mod_chunks=0, bias_of=None):
                h0 = HEAD[kind]
                ahead(first_unit + AHEAD)
                for t in range(HEADS + 3):
                    if t < HEADS:
                        g = h0 + t
                        p = head_cols(prob, g % SD)
                        st = stat[:, (g % SD) * 12:(g % SD + 1) * 12]
                        dve.wait_ge(sem("scores"), g + 1)
                        if g >= SD:
                            dve.wait_ge(sem("prob_turned"), g - SD + 1)
                        if kind == "moba":
                            dve.wait_ge(sem("alibi"), t + 1)
                        own, both = bias_of(t)
                        b = bank[t % 2]
                        dve.tensor_tensor_reduce(p[:, 0:P], b[:, 0:P], own, 1.0, NEG, ALU.add, ALU.max,
                                                 st[:, 0:1]).then_inc(sem("row_max"), 1)
                        dve.tensor_tensor_reduce(p[:, P:CAUSAL], b[:, P:CAUSAL], both, 1.0, NEG, ALU.add, ALU.max,
                                                 st[:, 1:2]).then_inc(sem("row_max"), 1)
                        dve.wait_ge(sem("row_max"), 2 * g + 2)
                        if kind == "swa":
                            link(dve.tensor_scalar(st[:, 10:12], st[:, 0:2], SCALE[kind], sinks[:, t:t + 1],
                                                   ALU.mult, ALU.max))
                            dve.tensor_scalar(st[:, 2:4], st[:, 10:12], -1.0, None, ALU.mult).then_inc(
                                sem("shifted"), 1)
                        else:
                            dve.tensor_scalar(st[:, 2:4], st[:, 0:2], -SCALE[kind], None, ALU.mult).then_inc(
                                sem("shifted"), 1)
                    if 1 <= t < HEADS + 1:
                        g = h0 + t - 1
                        p = head_cols(prob, g % SD)
                        st = stat[:, (g % SD) * 12:(g % SD + 1) * 12]
                        dve.wait_ge(sem("exped"), 2 * g + 2)
                        if kind == "swa":
                            dve.wait_ge(sem("sink_ready"), t)
                            link(dve.tensor_tensor(st[:, 4:6], st[:, 4:6], st[:, 8:10], ALU.add))
                        link(dve.reciprocal(st[:, 6:8], st[:, 4:6]))
                        dve.tensor_scalar(p[:, 0:P], p[:, 0:P], st[:, 6:7], None, ALU.mult).then_inc(
                            sem("prob_part"), 1)
                        dve.tensor_scalar(p[:, P:CAUSAL], p[:, P:CAUSAL], st[:, 7:8], None, ALU.mult).then_inc(
                            sem("prob_ready"), 1)
                    if t >= 3 and not pair:
                        h = t - 3
                        dve.wait_ge(sem("o_hi_ready"), h0 + h + 1)
                        dve.tensor_tensor(tiles(o_lo, h, h + 1), bank[(4, 7)[h % 2]][:, 0:S],
                                          tiles(o_hi, h, h + 1).bitcast(F32), ALU.subtract).then_inc(
                                              sem("o_ready"), 1)
                    if t < mod_chunks:
                        modulate(1)

            def ffn(l):
                w01 = pcol[f"conv_w{l}"]
                for i in range(FI):
                    n = l * FI + i
                    s = 2 * (n % 2)
                    product("ffa", l, i)
                    for t in range(2):
                        f = 2 * i + t
                        dve.wait_ge(sem("ff_c0"), 2 * n + 2)
                        c, a = tiles(conv, s + t, s + t + 1), bank[0][:, t * S:(t + 1) * S]
                        dve.scalar_tensor_tensor(c[:, 1:S], a[:, 0:S - 1], w01[:, FT + f:FT + f + 1], c[:, 1:S],
                                                 ALU.mult, ALU.add).then_inc(sem("ff_tap"), 1)
                    for t in range(2):
                        f = 2 * i + t
                        dve.wait_ge(sem("ff_tap"), 2 * n + t + 1)
                        c, a = tiles(conv, s + t, s + t + 1), bank[0][:, t * S:(t + 1) * S]
                        dve.scalar_tensor_tensor(c[:, 2:S], a[:, 0:S - 2], w01[:, f:f + 1], c[:, 2:S],
                                                 ALU.mult, ALU.add).then_inc(sem("ff_conv"), 1)
                    product("ffb", l, i)
                    dve.wait_ge(sem("ff_gelu"), n + 1)
                    dve.tensor_tensor(tiles(gated, s, s + 2), tiles(gated, s, s + 2), bank[1][:, :],
                                      ALU.mult).then_inc(sem("ff_gated"), 1)
                    dve.wait_ge(sem("ff_g_hi"), n + 1)
                    dve.tensor_tensor(tiles(o_lo, s, s + 2), tiles(gated, s, s + 2),
                                      tiles(o_hi, s, s + 2).bitcast(F32), ALU.subtract).then_inc(
                                          sem("ff_g_ready"), 1)
                    if i < KT:
                        modulate(2)
                product("ffo", l, FI - 1)
                dve.wait_ge(sem("x_ready"), 8 * (2 * l + 1))
                for m in range(KT):
                    residual(2 * l + 1, m, bank[4 + m // 2][:, (m % 2) * S:(m % 2 + 1) * S])

            def log1p(dst, e, t):
                a, b = t
                link(dve.tensor_scalar(a, e, 2.0, None, ALU.add))
                link(dve.reciprocal(a, a))
                link(dve.tensor_tensor(dst, e, a, ALU.mult))
                link(dve.tensor_tensor(a, dst, dst, ALU.mult))
                link(dve.tensor_scalar(b, a, 1.0 / 15, None, ALU.mult))
                for i in (13, 11, 9, 7, 5, 3):
                    link(dve.scalar_tensor_tensor(b, b, 1.0 / i, a, ALU.add, ALU.mult))
                link(dve.scalar_tensor_tensor(dst, b, 1.0, dst, ALU.add, ALU.mult))

            dve.memset(relb[BUCKETS:BUCKETS + 1, :], NEG).then_inc(sem("ones"), 1)
            dve.wait_ge(sem("pos_in"), 16 * 5)
            dve.wait_ge(sem("const_in"), 32)
            link(dve.tensor_copy(pos, pos_i))
            link(dve.tensor_copy(posq, posq_i[:, :]))
            link(dve.tensor_scalar(angle, pos, const(C_COL), None, ALU.mult))
            for dst, quarter in ((sin, 0.0), (cos, 0.25)):
                link(dve.tensor_scalar(turns, angle, 1 / (2 * np.pi), quarter, ALU.mult, ALU.add))
                link(dve.tensor_scalar(turns, turns, MAGIC, None, ALU.add))
                link(dve.tensor_scalar(turns, turns, -MAGIC, None, ALU.add))
                src = angle
                for part in TURN:
                    link(dve.scalar_tensor_tensor(dst, turns, -part, src, ALU.mult, ALU.add))
                    src = dst
                link(dve.tensor_scalar(dst, dst, quarter * 2 * np.pi, PI_DOWN, ALU.add, ALU.min))
                dve.tensor_scalar(dst, dst, -PI_DOWN, None, ALU.max).then_inc(sem("turned_angles"), 1)
            for t, (a, b) in enumerate(((0, P), (P, CAUSAL))):
                link(dve.tensor_scalar(dist[:, a:b], pos[:, 0:b - a], posq[:, t:t + 1], None, ALU.subtract))
                link(magnitude(dist[:, a:b], dist[:, a:b]))
                dve.tensor_tensor(dist[:, a:b], dist[:, a:b], mask[:, a:b], ALU.subtract).then_inc(
                    sem("dist_ready"), 1)
            dve.wait_ge(sem("c_act"), 1)
            modulate(8)
            ahead(AHEAD)
            fold(0, (2, 0))
            coefficients(0, mod8(0, 0), mod8(0, 1))
            for m in range(KT + 1):
                if m < KT:
                    dve.wait_ge(sem("x_copied"), m // 2 + 1)
                    h_full(0, m, tiles(x, m, m + 1))
                if m:
                    h_low(0, m - 1)

            for j in range(2):
                product("mla_in", j)
                modulate(1)
            product("mla_in", 2)
            for j in range(2):
                dve.wait_ge(sem("c_rooted"), j + 1)
                link(dve.reciprocal(tiles(rstd, j, j + 1), tiles(rstd, j, j + 1)))
                g = pcol["kv_norm" if j else "q_norm"]
                for m in range(2):
                    dve.scalar_tensor_tensor(tiles(hf, 2 * j + m, 2 * j + m + 1), bank[j][:, m * S:(m + 1) * S],
                                             g[:, m:m + 1], tiles(rstd, j, j + 1), ALU.mult,
                                             ALU.mult).then_inc(sem("c_full"), 1)
            for j in range(2):
                dve.wait_ge(sem("c_hi"), j + 1)
                dve.tensor_tensor(tiles(o_lo, 2 * j, 2 * j + 2), tiles(hf, 2 * j, 2 * j + 2),
                                  tiles(o_hi, 2 * j, 2 * j + 2).bitcast(F32), ALU.subtract).then_inc(
                                      sem("c_ready"), 1)
            dve.wait_ge(sem("rotary"), 2)
            dve.wait_ge(sem("kr_spread"), 1)
            link(dve.tensor_tensor(tiles(kk, 5, 6), bank[4][:, 0:S], cos, ALU.mult))
            link(dve.tensor_tensor(tiles(kk, 6, 7), bank[4][:, S:2 * S], sin, ALU.mult))
            link(dve.tensor_tensor(tiles(kk, 7, 8), tiles(kk, 5, 6), tiles(kk, 6, 7), ALU.add))
            link(dve.tensor_scalar(tiles(of, 6, 7), tiles(kk, 7, 8), half[0], None, ALU.mult))
            dve.tensor_scalar(tiles(of, 7, 8), tiles(kk, 7, 8), half[1], None, ALU.mult).then_inc(
                sem("kr_ready"), 1)
            for j in range(2):
                product("uq", j)
                modulate(3)
                dve.wait_ge(sem("q_swapped"), j + 1)
                link(dve.tensor_tensor(grid(tiles(kk, 8, 10), 2), grid(tiles(of, 4, 6), 2), row_times(cos, 2),
                                       ALU.mult))
                link(dve.tensor_tensor(grid(tiles(kk, 10, 12), 2), grid(bank[3][:, :], 2), row_times(sin, 2),
                                       ALU.mult))
                dve.tensor_tensor(tiles(of, 2 * j, 2 * j + 2), tiles(kk, 8, 10), tiles(kk, 10, 12),
                                  ALU.add).then_inc(sem("q_rotated"), 1)
                product("ukv", j)
            ahead(unit0("mla_o", 0) + AHEAD)
            fold(1, (5, 6))
            causal = lambda t: (mask[:, 0:P], mask[:, P:CAUSAL])
            attention("mla", False, unit0("mla_o", 0), 8, causal)
            fold(2, (0, 1))
            gate(0, mod8(1, 0), 1 / ALPHA)
            gate(1, mod8(2, 1), 1 / ALPHA)
            coefficients(1, mod8(1, 1), mod8(2, 0), pcol["ln_g"][:, 0:8], pcol["ln_b"][:, 0:8])
            out_projection("mla_o", 0)
            norm(0, 1)
            ffn(0)

            def moba_modulation():
                fold(3, (0, 1))
                coefficients(2, mod8(3, 0), mod8(3, 1), pcol["ln_g"][:, 8:16], pcol["ln_b"][:, 8:16])

            norm(1, 2, moba_modulation)

            for i in range(12):
                product("moba_in", i)
                if i == 1:
                    fold(4, (5, 6))
                    gate(2, mod8(4, 0), 1 / ALPHA)
                if 2 <= i < 10:
                    modulate(1)
            ahead(unit0("moba_o", 0) + AHEAD)
            fold(5, (5, 6))
            gate(3, mod8(5, 1), 1 / ALPHA)
            coefficients(3, mod8(4, 1), mod8(5, 0), pcol["ln_g"][:, 16:24], pcol["ln_b"][:, 16:24])
            attention("moba", False, unit0("moba_o", 0), 8,
                      lambda t: (alibi[t % 2][:, 0:P], alibi[t % 2][:, P:CAUSAL]))
            fold(6, (0, 1))
            coefficients(4, mod8(6, 0), mod8(6, 1), pcol["norm_g"][:, 0:8])
            dve.wait_ge(sem("x_ready"), 16)
            out_projection("moba_o", 2)
            norm(2, 3)
            ffn(1)
            norm(3, None)
            norm(4, 4)

            link(dve.memset(rstd[:, :], 0.0))
            product("a_kv", 0)
            product("f", 0)
            dve.wait_ge(sem("turn_read"), turn_of[("f", 0)] + 1)
            v = prob[0:16, 0:S]
            magnitude(prob[0:16, S:2 * S], v).then_inc(sem("f_abs"), 1)
            for m in range(2):
                product("a_q", m)
            fold(7, (5, 6))
            gate(4, mod8(7, 0), 1.0)
            gate(5, mod8(7, 1), 1.0)
            for m in range(2):
                product("b_q", m)
            fold(8, (5, 6))
            coefficients(5, mod8(8, 0), mod8(8, 1), pcol["norm_g"][:, 8:16])
            dve.wait_ge(sem("akv_turned"), 1)
            for at, src, h in ((0, tiles(kk, 8, 9), 0), (1, bank[4][:, 0:S], 1), (2, bank[4][:, 0:S], 0),
                               (3, tiles(kk, 8, 9), 1)):
                dve.tensor_scalar(tiles(kk, at, at + 1), src, half[h], None, ALU.mult).then_inc(
                    sem("akv_spread"), 1)
            dve.wait_ge(sem("vv_zero"), 1)
            for h in range(2):
                for side in range(2):
                    dst = vv[:, :].rearrange("p (t n f) -> p t n f", t=2, n=12)[:, :, 2 * h + side,
                                                                               side * 64:(side + 1) * 64]
                    src = bank[4][:, S:2 * S].rearrange("p (t f) -> p t f", t=2)[:, :, h * 64:(h + 1) * 64]
                    dve.tensor_copy(dst, src).then_inc(sem("akv_spread"), 1)
            dve.wait_ge(sem("f_exp"), 1)
            q, r = prob[0:16, 3 * S:4 * S], of[0:16, 0:S]
            log1p(q, prob[0:16, 2 * S:3 * S], (prob[0:16, S:2 * S], r))
            link(dve.tensor_scalar(v, v, 0.0, None, ALU.min))
            link(dve.scalar_tensor_tensor(v, q, -2.0, v, ALU.mult, ALU.add))
            link(dve.tensor_tensor_scan(rstd[0:16, 0:S], ones[0:16, 0:1].broadcast_to([16, S]), v, 0.0, ALU.mult,
                                        ALU.add))
            dve.tensor_scalar(rstd[:, S:2 * S], rstd[:, 0:S], const(C_COL + 4), const(C_COL + 5), ALU.mult,
                              ALU.add).then_inc(sem("decay_ready"), 1)
            for name in ("b_k", "b_v"):
                for m in range(2):
                    product(name, m)
            dve.wait_ge(sem("bias_in"), 16 * 8)
            attention("swa", True, unit0("a_gate", 0), 0,
                      lambda t: (tiles(bias, t, t + 1)[:, P:S], tiles(bias, t, t + 1)))
            for h in range(HEADS):
                dve.tensor_scalar(tiles(bias, h, h + 1), rstd[:, 0:S], const(C_SELF + h), const(C_SEL1 + h),
                                  ALU.mult, ALU.add).then_inc(sem("decay_ready"), 1)
            attention("fgt", True, unit0("a_gate", 0), 0, causal)
            for m in range(4):
                product("a_gate", m)
                dve.wait_ge(sem("turn_read"), turn_of[("a_gate", m)] + 1)
                dve.wait_ge(sem("pair_read"), 8)
                dve.tensor_tensor(tiles(of, 2 * m, 2 * m + 2), tiles(of, 2 * m, 2 * m + 2),
                                  prob[:, (m % 2) * 512:(m % 2 + 1) * 512], ALU.mult).then_inc(
                                      sem("head_gated"), 1)
                dve.wait_ge(sem("o_hi_ready"), 16 + m + 1)
                dve.tensor_tensor(tiles(o_lo, 2 * m, 2 * m + 2), tiles(of, 2 * m, 2 * m + 2),
                                  tiles(o_hi, 2 * m, 2 * m + 2).bitcast(F32), ALU.subtract).then_inc(
                                      sem("o_ready"), 1)
            out_projection("attn_o", 4)
            lam, lab, lex = pcol["lam"], small[:, 40:48], small[:, 48:56]
            magnitude(lab, lam).then_inc(sem("lam_abs"), 1)
            norm(5, 5)
            dve.wait_ge(sem("lam_exp"), 1)
            log1p(small[:, 56:64], lex, (small[:, 64:72], small[:, 72:80]))
            link(dve.tensor_scalar(small[:, 80:88], lam, -1.0, 0.0, ALU.mult, ALU.max))
            link(dve.scalar_tensor_tensor(small[:, 80:88], small[:, 56:64], 2.0, small[:, 80:88], ALU.mult, ALU.add))
            link(dve.tensor_scalar(lam8, small[:, 80:88], -LRU_C, None, ALU.mult))

            cw = pcol["conv2_w"]
            for m in range(4):
                product("xr", m)
                b = bank[turn_of[("xr", m)] % 4]
                for j in (2, 1, 0):
                    for t in range(2):
                        f = 2 * m + t
                        dve.wait_ge(sem("xc_started"), 2 * m + 2)
                        c, a = tiles(kk, f, f + 1), b[:, t * S:(t + 1) * S]
                        back = CONV2 - 1 - j
                        ins = dve.scalar_tensor_tensor(c[:, back:S], a[:, 0:S - back],
                                                       cw[:, 8 * j + f:8 * j + f + 1], c[:, back:S], ALU.mult,
                                                       ALU.add)
                        if j:
                            link(ins)
                        else:
                            ins.then_inc(sem("xc_full"), 1)
                dve.wait_ge(sem("xc_hi"), m + 1)
                dve.tensor_tensor(tiles(o_lo, 2 * m, 2 * m + 2), tiles(kk, 2 * m, 2 * m + 2),
                                  tiles(o_hi, 2 * m, 2 * m + 2).bitcast(F32), ALU.subtract).then_inc(
                                      sem("xc_ready"), 1)
                dve.nop().then_inc(sem("turn_read"), 1)
            product("w_a", 0)
            for n in range(KT):
                dve.wait_ge(sem("rg_read"), n + 1)
                dve.tensor_scalar(tiles(qz, n, n + 1), tiles(qz, n, n + 1), lam8[:, n:n + 1], None,
                                  ALU.mult).then_inc(sem("rate_ready"), 1)
            product("w_x", 0)
            ahead(unit0("l_gate", 0) + AHEAD)
            dve.wait_ge(sem("rg_read"), 16)
            for i in range(2):
                a, b = 4 * i, 4 * i + 4
                link(dve.tensor_tensor(tiles(vv, a, b), tiles(vv, a, b), tiles(kk, a, b), ALU.mult))
                dve.wait_ge(sem("rate_tanh"), i + 1)
                link(dve.tensor_scalar(tiles(of, a, b), tiles(bias, a, b), -1.0, 1.0, ALU.mult, ALU.add))
                link(dve.reciprocal(tiles(of, a, b), tiles(of, a, b)))
                dve.tensor_tensor(tiles(of, a, b), tiles(of, a, b), tiles(bias, a, b), ALU.mult).then_inc(
                    sem("ratio_ready"), 1)
            dve.nop().then_inc(sem("ix_ready"), 2)
            ahead(unit0("l_gate", 0) + 1 + AHEAD)
            for i in range(2):
                a, b = 4 * i, 4 * i + 4
                dve.wait_ge(sem("input_root"), i + 1)
                dve.wait_ge(sem("decay_exp"), i + 1)
                link(dve.tensor_tensor(tiles(vv, a, b), tiles(vv, a, b), tiles(of, a, b), ALU.mult))
                for m in range(4 * i, 4 * i + 4):
                    dve.tensor_tensor_scan(tiles(bias, m, m + 1), tiles(qz, m, m + 1), tiles(vv, m, m + 1), 0.0,
                                           ALU.mult, ALU.add).then_inc(sem("scanned"), 1)
            for m in range(4):
                product("l_gate", m)
                dve.wait_ge(sem("turn_read"), turn_of[("l_gate", m)] + 1)
                dve.wait_ge(sem("scanned"), 2 * m + 2)
                dve.tensor_tensor(tiles(kk, 2 * m, 2 * m + 2), tiles(kk, 2 * m, 2 * m + 2),
                                  tiles(bias, 2 * m, 2 * m + 2), ALU.mult).then_inc(sem("l_gated"), 1)
                dve.wait_ge(sem("o_hi_ready"), 20 + m + 1)
                dve.tensor_tensor(tiles(o_lo, 2 * m, 2 * m + 2), tiles(kk, 2 * m, 2 * m + 2),
                                  tiles(o_hi, 2 * m, 2 * m + 2).bitcast(F32), ALU.subtract).then_inc(
                                      sem("o_ready"), 1)
            out_projection("lru_o", 5)
            norm(6, None)


INPUTS = ["x", "c", "positions", "mod_w", "mod_b", "ln_g", "ln_b", "ffn_w_in", "ffn_conv_w", "ffn_conv_b",
          "ffn_w_out", "mla_w_in", "mla_q_norm", "mla_w_uq", "mla_kv_norm", "mla_w_ukv", "mla_w_o", "moba_w_in",
          "moba_w_o", "c_2", "rel_bias_2", "norm_g_2", "ada_w_2", "ada_b_2", "attn_w_in_2", "attn_sinks_2",
          "attn_b_f_2", "attn_w_out_2", "lru_w_in_2", "lru_conv_w_2", "lru_conv_b_2", "lru_w_a_2", "lru_b_a_2",
          "lru_w_x_2", "lru_b_x_2", "lru_lambda_2", "lru_w_out_2", "final_g_2"]


def kernel(**inputs):
    import concourse.bacc as bacc
    from concourse.bass_utils import run_bass_kernel_spmd

    nc = bacc.Bacc("TRN2", target_bir_lowering=False, num_devices=1)
    arrays, w = {}, {}
    for name in INPUTS:
        a = np.ascontiguousarray(inputs[name])
        arrays[f"in_{name}"] = a
        w[name] = nc.dram_tensor(f"in_{name}", a.shape, mybir.dt.from_np(a.dtype), kind="ExternalInput").ap()
    table = constants()
    arrays["in_constants"] = table
    consts = nc.dram_tensor("in_constants", table.shape, F32, kind="ExternalInput").ap()
    out = nc.dram_tensor("out_x", (1, S, D), F32, kind="ExternalOutput").ap()
    build(nc, w, consts, out)
    r = run_bass_kernel_spmd(nc, [arrays], core_ids=[0])
    return r.results[0]["out_x"]
```

```python
from contextlib import ExitStack

import numpy as np

import concourse.bass as bass
from concourse import mybir

P = 128
D = 1024
KT = D // P
S = 256
QB = S // P
DFF = 2816
FT = DFF // P
FI = FT // 2
HEADS = 8
NOPE, ROPE, VD = 128, 64, 128
MLA_RANK = 256
HD2 = 64
CONV2 = 4
BUCKETS, EXACT, MAXDIST = 32, 16, 128
ALPHA = 4.0 ** 0.25
LN_EPS, RMS_EPS = 1e-5, 1e-6
NEG = -1e30
CAUSAL = P + S
LRU_C = 8.0
MAGIC = 1.5 * 2.0 ** 23
_a = np.float32(np.floor(2 * np.pi * 2 ** 8) / 2 ** 8)
_b = np.float32(np.floor((2 * np.pi - float(_a)) * 2 ** 19) / 2 ** 19)
TURN = [float(_a), float(_b), float(np.float32(2 * np.pi - float(_a) - float(_b)))]
PI_DOWN = float(np.nextafter(np.float32(np.pi), np.float32(0)))

ALU = mybir.AluOpType
ACT = mybir.ActivationFunctionType
AX = mybir.AxisListType
F32 = mybir.dt.float32
F32R = mybir.dt.float32r
I32 = mybir.dt.int32

RAW = 3
UNITS = 6
UL = 1024
AHEAD = UNITS - 1
MODRAW = 2
LRU_EARLY = 1
SD = 3

C_ID, C_SWAP32, C_SWAP64, C_DUP, C_DUPS = (i * P for i in range(5))
C_MASK = 5 * P
C_COL = C_MASK + CAUSAL
C_SELF, C_SEL1 = C_COL + 6, C_COL + 14
C_BUCKET = C_COL + 22
C_END = C_BUCKET + 2 * S

PB = [
    [("c", 8), ("c_2", 8), ("q_norm", 2), ("kv_norm", 2), ("norm_g", 16), ("final_g", 8), ("conv2_w", 32),
     ("conv2_b", 8), ("b_a", 8), ("b_x", 8), ("lam", 8)],
    [("mod_b", 96)],
    [("ada_b", 48), ("ln_g", 32), ("ln_b", 32)],
    [("conv_w0", 66), ("conv_b0", 22)],
    [("conv_w1", 66), ("conv_b1", 22)],
]


def constants():
    c = np.zeros((P, C_END), np.float32)
    i = np.arange(P)
    c[i, C_ID + i] = 1
    c[:, C_MASK:C_MASK + P] = np.where(i[None] <= i[:, None], 0, NEG)
    c[:, C_MASK + 2 * P:C_MASK + 3 * P] = c[:, C_MASK:C_MASK + P]
    c[i, C_SWAP32 + (i ^ 32)] = 1
    c[i, C_SWAP64 + (i ^ 64)] = 1
    j = np.arange(64)
    for h in range(2):
        c[j, C_DUP + 64 * h + j] = 1
        c[j, C_DUPS + 64 * h + (j ^ 32)] = 1
    c[:, C_COL] = (np.float32(10000.0) ** (-np.arange(32, dtype=np.float32) / 32))[i % 32]
    c[:, C_COL + 1] = np.where((i // 32) % 2 == 0, -1, 1)
    c[:, C_COL + 2] = i < 64
    c[:, C_COL + 3] = i >= 64
    dist = 255 - np.arange(2 * S)
    n = np.maximum(dist, 1)
    large = EXACT + (np.log(n / EXACT) / np.log(MAXDIST / EXACT) * (BUCKETS - EXACT)).astype(int)
    bucket = np.where(dist < EXACT, np.maximum(dist, 0), np.minimum(large, BUCKETS - 1))
    ok = (dist >= 0) & (dist < P)
    for b in range(BUCKETS):
        c[b, C_BUCKET:C_BUCKET + 2 * S] = (bucket == b) & ok
    c[BUCKETS, C_BUCKET:C_BUCKET + 2 * S] = ~ok
    root = HD2 ** 0.5
    c[0:8, C_COL + 4] = root
    c[8:16, C_COL + 5] = 1
    for h in range(8):
        c[8 + h, C_SELF + h] = -root
        c[h, C_SEL1 + h] = 1
    return c


def weight_stream(w):
    out = []

    def cols(key, src, n0, n=256, copies=1):
        out.append((key, [(src[:, n0:n0 + n].rearrange("(k p) c -> p k c", p=P), i * n) for i in range(copies)],
                    n * copies))

    def ffn(i):
        for it in range(FI + 1):
            if it < FI:
                cols(("ffa", i, it), w["ffn_w_in"][i], it * 256)
                cols(("ffb", i, it), w["ffn_w_in"][i], DFF + it * 256)
            if it:
                src = w["ffn_w_out"][i][(it - 1) * 256:it * 256, :]
                out.append((("ffo", i, it - 1), [(src.rearrange("(k p) c -> p k c", p=P), 0)], 1024))

    mla_in = w["mla_w_in"][0]
    cols(("mla_in", 0), mla_in, 0)
    cols(("mla_in", 1), mla_in, 256)
    cols(("mla_in", 2), mla_in, 512, 64)
    for j in range(2):
        for name, width in (("uq", 768), ("ukv", 1024)):
            src = w[f"mla_w_{name}"][0][:, j * width:(j + 1) * width]
            if name == "uq":
                src = src.rearrange("(k p) (h c) -> p k h c", p=P, h=4)
                out.append(((name, j), [(src[:, k:k + 1, :, a:b], at) for k in range(2)
                                        for a, b, at in ((0, NOPE, 0), (NOPE, NOPE + ROPE, 4 * NOPE))], width))
            else:
                out.append(((name, j), [(src.rearrange("(k p) c -> p k c", p=P), 0)], width))
    for m in range(4):
        cols(("mla_o", m), w["mla_w_o"][0], m * 256)
    ffn(0)
    for part in range(3):
        for m in range(4):
            cols(("moba_in", part * 4 + m), w["moba_w_in"][0], part * 1024 + m * 256)
    for m in range(4):
        cols(("moba_o", m), w["moba_w_o"][0], m * 256)
    ffn(1)
    ain = w["attn_w_in_2"][0]
    cols(("a_kv", 0), ain, 512)
    cols(("f", 0), ain, 2304, 8, 2)
    for m in range(2):
        cols(("a_q", m), ain, m * 256)
    for m in range(2):
        cols(("b_q", m), ain, 768 + m * 256)
    for m in range(2):
        cols(("b_k", m), ain, 1280 + m * 256)
    for m in range(2):
        cols(("b_v", m), ain, 1792 + m * 256)
    for m in range(4):
        cols(("a_gate", m), ain, 2312 + m * 256)
    for m in range(4):
        cols(("attn_o", m), w["attn_w_out_2"][0], m * 256)
    lin = w["lru_w_in_2"][0]
    for m in range(4):
        cols(("xr", m), lin, m * 256)
    for m in range(LRU_EARLY):
        cols(("l_gate", m), lin, 1024 + m * 256)
    for name in ("a", "x"):
        out.append(((f"w_{name}", 0), [(w[f"lru_w_{name}_2"][0].rearrange("n w v -> w n v"), 0)], 128))
    for m in range(LRU_EARLY, 4):
        cols(("l_gate", m), lin, 1024 + m * 256)
    for m in range(4):
        cols(("lru_o", m), w["lru_w_out_2"][0], m * 256)
    return out


def modulation_stream(w):
    mod, ada = w["mod_w"], w["ada_w_2"]
    out = []

    def rows(g, parts):
        for k in range(KT):
            out.append((g, k, [(src[k * P:(k + 1) * P, a:b], at) for src, a, b, at in parts]))

    groups = [
        [(mod[0], 0, 2048, 0)], [(mod[0], 2048, 4096, 0)], [(mod[0], 4096, 5120, 0)], [(mod[0], 5120, 6144, 0)],
        [(mod[1], 0, 2048, 0)], [(mod[1], 2048, 4096, 0)], [(mod[1], 4096, 6144, 0)],
        [(ada[0], 0, 2048, 0)],
        [(ada[0], 2048, 3072, 0), (ada[1], 2048, 3072, 1024)],
        [(ada[1], 0, 2048, 0)],
    ]
    for g in (0, 1, 2):
        rows(g, groups[g])
    for k in range(KT):
        for g in (3, 4):
            out.append((g, k, [(src[k * P:(k + 1) * P, a:b], at) for src, a, b, at in groups[g]]))
    for g in range(5, len(groups)):
        rows(g, groups[g])
    return out


def build(nc, w, consts, out):
    chunks = weight_stream(w)
    chunk_of = {key: n for n, (key, _, _) in enumerate(chunks)}
    row_tiles = [2 if key[0] in ("uq", "ukv", "ffo") else KT for key, _, _ in chunks]
    length = [k * width for k, (_, _, width) in zip(row_tiles, chunks)]
    mods = modulation_stream(w)
    NU = 2 * len(chunks)

    def unit0(*key):
        return 2 * chunk_of[key]

    landed, count = [], [0] * RAW
    for n, (_, parts, _) in enumerate(chunks):
        count[n % RAW] += 16 * len(parts)
        landed.append(count[n % RAW])
    early = range(MODRAW, MODRAW + RAW + 1)
    mod_slot = [n % MODRAW for n in range(len(mods))]
    mod_landed, count = [], [0] * MODRAW
    for n, (_, _, parts) in enumerate(mods):
        if n in early:
            mod_landed.append(16)
        else:
            count[mod_slot[n]] += 16 * len(parts)
            mod_landed.append(count[mod_slot[n]])

    with ExitStack() as ctx:
        def sb(name, shape, dt=F32):
            return ctx.enter_context(nc.sbuf_tensor(name, shape, dt))

        sems = {}

        def sem(name):
            if name not in sems:
                sems[name] = ctx.enter_context(nc.semaphore(name))
            return sems[name]

        raw = sb("raw", [P, RAW, 2 * UL])
        modraw = sb("modraw", [P, MODRAW, 2048])
        w_hi = sb("w_hi", [P, UNITS, UL], F32R)
        w_lo = sb("w_lo", [P, UNITS, UL], F32R)
        h_hi = sb("h_hi", [P, KT * S], F32R)
        h_lo = sb("h_lo", [P, KT * S], F32R)
        o_hi = sb("o_hi", [P, KT * S], F32R)
        o_lo = sb("o_lo", [P, KT * S], F32R)
        x = sb("x", [P, KT * S])
        modsum = sb("modsum", [P, 2048])
        qz = sb("qz", [P, KT * S])
        kk = sb("kk", [P, 12 * S])
        vv = sb("vv", [P, 2 * 12 * P])
        of = sb("of", [P, KT * S])
        bias = sb("bias", [P, 8 * S])
        prob = sb("prob", [P, SD * CAUSAL])
        probT = sb("probT", [P, 2 * CAUSAL])
        cst = sb("cst", [P, C_BUCKET])
        cols = sb("cols", [P, 5 * P])
        modc = sb("modc", [P, 10 * 16])
        lncol = sb("lncol", [P, 12 * KT])
        gates = sb("gates", [P, 6 * KT])
        ones = sb("ones", [P, P])
        stat = sb("stat", [P, SD * 12])
        sinks = sb("sinks", [P, 8])
        small = sb("small", [P, 96])
        bf = sb("bf", [16, 1])
        rstd = sb("rstd", [P, 2 * S])
        relb = sb("relb", [BUCKETS + 1, 8])
        posq_i = sb("posq_i", [P, 2], I32)
        ebias = nc.dram_tensor("ebias", [8, P, CAUSAL], F32, kind="Internal").ap()
        bank = [ctx.enter_context(nc.psum_tensor(f"bank{i}", [P, 512], F32)) for i in range(8)]

        def tiles(t, a, b):
            return t[:, a * S:b * S]

        def grid(ap, n):
            return ap.rearrange("p (n s) -> p n s", n=n)

        def row_times(ap, n):
            return ap.rearrange("p (n s) -> p n s", n=1).broadcast_to([P, n, S])

        def head_cols(t, n):
            return t[:, n * CAUSAL:(n + 1) * CAUSAL]

        def const(at, n=1):
            return cst[:, at:at + n]

        def vtile(t, n, a=0, b=P):
            return vv[:, (t * 12 + n) * P + a:(t * 12 + n) * P + b]

        prow = kk[:, 0:5 * P]
        xrow = of[:, :]
        cos, sin, pos, angle = (tiles(bias, i, i + 1) for i in (0, 1, 6, 7))
        dist = bias[:, 2 * S:2 * S + CAUSAL]
        turns = bias[:, 4 * S:5 * S]
        pos_i = qz[:, 0:S].bitcast(I32)
        alibi = [vv[:, (t * 12 + 8) * P:(t * 12 + 8) * P + CAUSAL] for t in range(2)]
        mask = const(C_MASK, CAUSAL)
        ident = const(C_ID, P)
        half = [const(C_COL + 2), const(C_COL + 3)]
        hf = kk[:, 8 * S:12 * S]
        conv = kk[:, 8 * S:12 * S]
        gated = kk[:, 4 * S:8 * S]
        modacc = [of[:, :] if g in (3, 5, 7) else kk[:, 8 * S:12 * S] if g == 2 else modsum[:, :] for g in range(10)]
        mod_width = [max(sum(src.shape[1] for src, _ in parts) for h, _, parts in mods if h == g) for g in range(10)]
        mod_end = [1 + max(n for n, (h, _, _) in enumerate(mods) if h == g) for g in range(10)]
        parts_before = [sum(mod_width[:g]) // (4 * P) for g in range(10)]
        pcol = {}
        for b, rows in enumerate(PB):
            at = b * P
            for name, n in rows:
                pcol[name] = cols[:, at:at + n]
                at += n
        c_act = small[:, 0:16]
        lam8 = small[:, 16:24]
        posq = small[:, 24:26]

        def unit_ap(ring, u):
            n = u // 2
            half_len = length[n] // 2
            return ring[:, (u % UNITS) * UL:(u % UNITS) * UL + half_len]

        w_hi_f, w_lo_f = w_hi[:, :, :].rearrange("p a b -> p (a b)"), w_lo[:, :, :].rearrange("p a b -> p (a b)")

        def hi(u):
            return unit_ap(w_hi_f, u)

        def lo(u):
            return unit_ap(w_lo_f, u)

        def raw_unit(u):
            n = u // 2
            half_len = length[n] // 2
            return raw[:, n % RAW, (u % 2) * half_len:(u % 2 + 1) * half_len]

        HEAD = {"mla": 0, "moba": 8, "swa": 16, "fgt": 24}
        SCALE = {"mla": (NOPE + ROPE) ** -0.5, "moba": 128 ** -0.5, "swa": HD2 ** -0.5, "fgt": HD2 ** -0.5}
        turn_keys = [("moba_in", i) for i in range(12)]
        turn_keys += [("a_kv", 0), ("f", 0)] + [(n, m) for n in ("a_q", "b_q", "b_k", "b_v") for m in range(2)]
        turn_keys += [("a_gate", m) for m in range(4)] + [("xr", m) for m in range(4)]
        turn_keys += [("l_gate", m) for m in range(4)]
        turn_of = {key: n for n, key in enumerate(turn_keys)}

        def early_slot(n):
            return raw[:, n - MODRAW, :] if n < MODRAW + RAW else vv[:, 0:2048]

        block = ctx.enter_context(nc.Block())

        @block.sync
        def _(sp):
            for i, name in enumerate(("c", "c_2")):
                sp.dma_start(prow[8 * i:8 * i + 8, 0:P],
                             w[name].rearrange("a (n q) -> (a n) q", q=P)).then_inc(sem("c_in"), 16)
            sp.dma_start(cst[:, C_ID:C_ID + P], consts[:, C_ID:C_ID + P]).then_inc(sem("ident_in"), 16)
            sp.dma_start(pos_i, w["positions"].broadcast_to([P, S])).then_inc(sem("pos_in"), 16)
            sp.dma_start(posq_i[:, :], w["positions"][0].rearrange("(t p) -> p t", p=P), allow_slow_non_contiguous=True).then_inc(sem("pos_in"), 16)
            sp.dma_start(cst[:, P:C_BUCKET], consts[:, P:C_BUCKET]).then_inc(sem("const_in"), 16)
            sp.dma_start(prob[0:BUCKETS + 1, 0:2 * S],
                         consts[0:BUCKETS + 1, C_BUCKET:C_END]).then_inc(sem("buckets_in"), 16)
            for n in early:
                sp.dma_start(early_slot(n), mods[n][2][0][0]).then_inc(sem(f"mod_early{n}"), 16)
            sp.dma_start(xrow.rearrange("p (t f) -> p t f", t=2),
                         w["x"][0].rearrange("(t p) f -> p t f", p=P)).then_inc(sem("x_in"), 16)
            sp.dma_start(sinks[:, :], w["attn_sinks_2"].broadcast_to([P, 8])).then_inc(sem("attn_in"), 16)
            for i in range(2):
                sp.dma_start(bf[8 * i:8 * i + 8, :], w["attn_b_f_2"].rearrange("a b -> b a"), allow_slow_non_contiguous=True).then_inc(
                    sem("attn_in"), 16)
            for n, (key, parts, width) in enumerate(chunks):
                if n < RAW:
                    sp.wait_ge(sem("mod_summed"), early[n] + 1)
                else:
                    sp.wait_ge(sem("w_lo_ready"), 2 * (n - RAW) + 2)
                dst = raw[:, n % RAW, 0:length[n]].rearrange("p (k c) -> p k c", c=width)
                for i, (src, at) in enumerate(parts):
                    if key[0] == "uq":
                        to = dst[:, i // 2, at:at + 4 * src.shape[3]].rearrange("p (h c) -> p h c", h=4)
                        sp.dma_start(to, src[:, 0]).then_inc(sem(f"w_in{n % RAW}"), 16)
                    else:
                        sp.dma_start(dst[:, :, at:at + src.shape[2]], src).then_inc(sem(f"w_in{n % RAW}"), 16)
            for t in range(2):
                sp.wait_ge(sem("out_rows"), 2 * t + 2)
                sp.dma_start(out[0, t * P:(t + 1) * P, :], kk[:, t * D:(t + 1) * D]).then_inc(sem("stored"), 16)
            sp.wait_ge(sem("stored"), 32)

        N_PARAM = sum(len(rows) for rows in PB) - 2

        @block.gpsimd
        def _(pool):
            pool.memset(ones[:, :], 1.0).then_inc(sem("ones"), 1)

            def modulation(a, b):
                for n in range(a, b):
                    slot = mod_slot[n]
                    if n > MODRAW:
                        last = n - MODRAW if n - MODRAW not in early else slot
                        pool.wait_ge(sem("mod_summed"), last + 1)
                    for src, at in mods[n][2]:
                        pool.dma_start(modraw[:, slot, at:at + src.shape[1]], src).then_inc(
                            sem(f"mod_in{slot}"), 16)

            modulation(0, MODRAW)
            pool.dma_start(relb[0:BUCKETS, :], w["rel_bias_2"]).then_inc(sem("relb_in"), 16)
            modulation(early[-1] + 1, KT)
            pool.wait_ge(sem("bias_row"), 1)
            pool.dma_start(ebias, probT[0:8, 0:CAUSAL].rearrange("h (q j) -> h q j", q=1).broadcast_to(
                [8, P, CAUSAL])).then_inc(sem("ebias_out"), 16)
            modulation(KT, 4 * KT)
            pool.wait_ge(sem("dist_ready"), 2)

            def alibi_table(h):
                if h >= 2:
                    pool.wait_ge(sem("shifted"), 8 + h - 1)
                pool.tensor_scalar(alibi[h % 2], dist, -(2.0 ** -(h + 1)) / SCALE["moba"], None,
                                   ALU.mult).then_inc(sem("alibi"), 1)

            alibi_table(0)
            alibi_table(1)
            modulation(4 * KT, 7 * KT - 1)
            for h in range(2, HEADS):
                alibi_table(h)
                if h in (4, 7):
                    n = 7 * KT - 1 + (h - 4) // 3
                    modulation(n, n + 1)
            modulation(7 * KT + 1, 7 * KT + 2)
            pool.wait_ge(sem("head_out"), 16)
            pool.memset(vv[:, :], 0.0).then_inc(sem("vv_zero"), 1)
            pool.wait_ge(sem("ebias_out"), 16)
            pool.wait_ge(sem("alibi"), 8)
            pool.wait_ge(sem("q_rotated"), 2)
            for h in range(8):
                src = bass.AP(ebias.tensor, h * P * CAUSAL + P - 1, [[CAUSAL - 1, P], [1, S]])
                pool.dma_start(tiles(bias, h, h + 1), src).then_inc(sem("bias_in"), 16)
            modulation(7 * KT + 2, len(mods))
            for i in range(2):
                pool.wait_ge(sem("rg_read"), 8 + 4 * i + 4)
                pool.wait_ge(sem("xc_ready"), 4)
                pool.tensor_tensor(tiles(vv, 4 * i, 4 * i + 4), tiles(vv, 4 * i, 4 * i + 4),
                                   tiles(kk, 4 * i, 4 * i + 4), ALU.mult).then_inc(sem("ix_ready"), 1)

        @block.tensor
        def _(pe):
            fold_n = [0]

            def start_unit(u):
                pe.wait_ge(sem("w_hi_ready"), u + 1)
                pe.wait_ge(sem("w_lo_ready"), u + 1)

            def feature_product(dst, u, cut, a_hi, a_lo, first, last):
                pe.matmul(dst, cut(hi(u)), a_hi, start=first, stop=False, skip_group_check=True)
                pe.matmul(dst, cut(hi(u)), a_lo, start=False, stop=False, skip_group_check=True)
                return pe.matmul(dst, cut(lo(u)), a_hi, start=False, stop=last, skip_group_check=True)

            def token_product(dst, u, cut, a_hi, a_lo, first, last):
                pe.matmul(dst, a_hi, cut(hi(u)), start=first, stop=False, skip_group_check=True)
                pe.matmul(dst, a_hi, cut(lo(u)), start=False, stop=False, skip_group_check=True)
                return pe.matmul(dst, a_lo, cut(hi(u)), start=False, stop=last, skip_group_check=True)

            def columns_chunk(key, dst, a, width=256, e=None, heads=None):
                u0 = unit0(*key)
                step = min(width, P)
                for u in (u0, u0 + 1):
                    start_unit(u)
                    for k in range(4):
                        kt = 4 * (u - u0) + k
                        if e is not None:
                            pe.wait_ge(sem("h_ready"), 8 * e + kt + 1)
                        if heads is not None:
                            pe.wait_ge(sem("o_ready"), heads[kt])
                        for f in range(width // step):
                            at = k * width + f * step
                            ins = feature_product(dst[0:step, f * S:(f + 1) * S], u,
                                                  lambda r: r[:, at:at + step], tiles(a[0], kt, kt + 1),
                                                  tiles(a[1], kt, kt + 1), kt == 0 and f == 0, kt == KT - 1)
                    if u == u0:
                        ins.then_inc(sem("w_used"), 1)
                return ins

            def end_chunk(ins):
                ins.then_inc(sem("w_used"), 1)

            def turn(key):
                n = turn_of[key]
                if n >= 4:
                    pe.wait_ge(sem("turn_read"), n - 3)
                return bank[n % 4]

            def fold(g, b, parts=range(4)):
                pe.wait_ge(sem("mod_summed"), mod_end[g])
                for part in parts[:mod_width[g] // (4 * P)]:
                    n = fold_n[0]
                    if n >= 2:
                        pe.wait_ge(sem("fold_summed"), n - 1)
                    for i in range(4):
                        at = (4 * part + i) * P
                        ins = pe.transpose(bank[b[n % 2]][:, i * P:(i + 1) * P], modacc[g][:, at:at + P], ident)
                    ins.then_inc(sem("fold_turned"), 1)
                    fold_n[0] += 1

            def norm_sums(n, centered=True):
                if centered:
                    for m in range(KT):
                        pe.wait_ge(sem("z_ready"), 8 * n + m + 1)
                        ins = pe.matmul(bank[3][:, 0:S], ones[:, :], tiles(qz, m, m + 1), start=m == 0, stop=m == 7)
                    ins.then_inc(sem("mean_done"), 1)
                for m in range(KT):
                    pe.wait_ge(sem("squared"), 8 * n + m + 1)
                    ins = pe.matmul(bank[2][:, 0:S], ones[:, :], tiles(kk, m, m + 1), start=m == 0, stop=m == 7)
                ins.then_inc(sem("var_done"), 1)

            def attention(kind, scores, value, pair):
                h0 = HEAD[kind]
                for t in range(HEADS + 3):
                    if t < HEADS:
                        g = h0 + t
                        if t >= 2:
                            pe.wait_ge(sem("shifted"), g - 1)
                        b = bank[t % 2]
                        ops = scores(t)
                        for i, (q, k) in enumerate(ops):
                            pe.matmul(b[:, 0:P], q[:, 0:P], k[:, 0:P], start=i == 0, stop=i == len(ops) - 1,
                                      skip_group_check=True)
                        for i, (q, k) in enumerate(ops):
                            ins = pe.matmul(b[:, P:CAUSAL], q[:, P:S], k[:, 0:S], start=False,
                                            stop=i == len(ops) - 1, skip_group_check=True)
                        ins.then_inc(sem("scores"), 1)
                    if 2 <= t < HEADS + 2:
                        g = h0 + t - 2
                        pe.wait_ge(sem("prob_ready"), g + 1)
                        if t >= 4:
                            pe.wait_ge(sem("probT_ready"), g - 1)
                        b = bank[2 + t % 2]
                        for i in range(3):
                            ins = pe.transpose(b[:, i * P:(i + 1) * P],
                                               prob[:, (g % SD) * CAUSAL + i * P:(g % SD) * CAUSAL + (i + 1) * P],
                                               ident)
                        ins.then_inc(sem("prob_turned"), 1)
                    if t >= 3:
                        h = t - 3
                        g = h0 + h
                        pe.wait_ge(sem("probT_ready"), g + 1)
                        n = (h // 2 if pair else h)
                        if n >= 2 and not (pair and h % 2):
                            pe.wait_ge(sem("pair_read" if pair else "o_ready"), outs0[kind] + n - 1)
                        dst = bank[(4, 7)[n % 2]][:, 0:S]
                        pt = head_cols(probT, g % 2)
                        first = not (pair and h % 2)
                        pe.matmul(dst, value(h, 0), pt[:, 0:S], start=first, stop=False, skip_group_check=True)
                        ins = pe.matmul(dst[:, P:S], value(h, 1), pt[:, S:CAUSAL], start=False, stop=True,
                                        skip_group_check=True)
                        ins.then_inc(sem("head_out"), 1)

            outs0 = {"mla": 0, "moba": 8, "swa": 0, "fgt": 4}

            heads = {"mla_o": [kt + 1 for kt in range(KT)], "moba_o": [8 + kt + 1 for kt in range(KT)],
                     "attn_o": [16 + kt // 2 + 1 for kt in range(KT)],
                     "lru_o": [20 + kt // 2 + 1 for kt in range(KT)]}
            residual = {"mla_o": 0, "moba_o": 2, "attn_o": 4, "lru_o": 5}

            def out_projection(name, g=None):
                for m in range(4):
                    if m == 3 and g is not None:
                        fold(g, (0, 1))
                    if m >= 2:
                        pe.wait_ge(sem("z_ready"), 8 * residual[name] + 2 * (m - 1))
                    end_chunk(columns_chunk((name, m), bank[5 + m % 2], (o_hi, o_lo),
                                            heads=None if m else heads[name]))

            def ffn(l):
                for i in range(FI + 1):
                    n = l * FI + i
                    if i < FI:
                        if n:
                            pe.wait_ge(sem("ff_conv"), 2 * n)
                        end_chunk(columns_chunk(("ffa", l, i), bank[0], (h_hi, h_lo),
                                                e=None if i else (1, 3)[l]))
                        if n:
                            pe.wait_ge(sem("ff_gated"), n)
                        end_chunk(columns_chunk(("ffb", l, i), bank[1], (h_hi, h_lo)))
                    if l == 0 and i == FI - 3:
                        fold(3, (2, 3))
                    if i in (FI - 2, FI - 1):
                        fold((4, 7)[l], (2, 3), (0, 1) if i == FI - 2 else (2, 3))
                    if i:
                        u0 = unit0("ffo", l, i - 1)
                        pe.wait_ge(sem("ff_g_ready"), n)
                        for u in (u0, u0 + 1):
                            start_unit(u)
                            k = 2 * ((n - 1) % 2) + u - u0
                            for m in range(KT):
                                first = i == 1 and u == u0 and m % 2 == 0
                                ins = feature_product(bank[4 + m // 2][:, (m % 2) * S:(m % 2 + 1) * S], u,
                                                      lambda r: r[:, m * P:(m + 1) * P], tiles(o_hi, k, k + 1),
                                                      tiles(o_lo, k, k + 1), first, i == FI and u > u0)
                            ins.then_inc(sem("w_used"), 1)

            pe.wait_ge(sem("ident_in"), 16)
            pe.wait_ge(sem("c_in"), 32)
            pe.transpose(bank[3][:, 0:16], prow[0:16, 0:P], cst[0:16, C_ID:C_ID + 16]).then_inc(sem("c_turned"), 1)
            pe.wait_ge(sem("const_in"), 16)
            pe.wait_ge(sem("buckets_in"), 16)
            pe.wait_ge(sem("ones"), 2)
            pe.wait_ge(sem("params_in"), 16 * N_PARAM)
            for b, rows in enumerate(PB):
                n = sum(r[1] for r in rows)
                ins = pe.transpose(bank[b // 4][:, (b % 4) * P:(b % 4) * P + n], prow[0:n, b * P:(b + 1) * P],
                                   cst[0:n, C_ID:C_ID + n])
            ins.then_inc(sem("params_turned"), 1)
            pe.wait_ge(sem("x_in"), 16)
            for m in range(KT):
                for t in range(2):
                    at = (m % 2) * S + t * P
                    ins = pe.transpose(bank[4 + m // 2][:, at:at + P], xrow[:, t * D + m * P:t * D + (m + 1) * P],
                                       ident)
                ins.then_inc(sem("x_turned"), 1)
            pe.wait_ge(sem("c_act"), 1)
            pe.wait_ge(sem("relb_in"), 16)
            pe.matmul(bank[3][0:8, :], relb[:, :], prob[0:BUCKETS + 1, 0:2 * S], start=True,
                      stop=True).then_inc(sem("bias_turned"), 1)
            pe.wait_ge(sem("cols_ready"), 5)
            fold(0, (2, 0))

            for j in range(2):
                end_chunk(columns_chunk(("mla_in", j), bank[j], (h_hi, h_lo), e=None if j else 0))
            pe.wait_ge(sem("fold_summed"), 4)
            pe.wait_ge(sem("bias_row"), 1)
            for j in range(2):
                if j:
                    end_chunk(columns_chunk(("mla_in", 2), bank[2], (h_hi, h_lo), 64))
                pe.wait_ge(sem("c_squared"), j + 1)
                if j:
                    pe.wait_ge(sem("c_rooted"), 1)
                for m in range(2):
                    ins = pe.matmul(bank[3][:, j * S:(j + 1) * S], ones[:, :], tiles(kk, 2 * j + m, 2 * j + m + 1),
                                    start=m == 0, stop=m == 1)
                ins.then_inc(sem("c_summed"), 1)
            pe.wait_ge(sem("kr_copied"), 1)
            pe.wait_ge(sem("x_copied"), 4)
            for i, at in enumerate((C_DUP, C_DUPS)):
                ins = pe.matmul(bank[4][:, i * S:(i + 1) * S], cst[0:64, at:at + P], tiles(kk, 4, 5)[0:64, :],
                                start=True, stop=True)
            ins.then_inc(sem("kr_spread"), 1)
            for j in range(2):
                u0 = unit0("uq", j)
                pe.wait_ge(sem("c_ready"), 2)
                if j:
                    pe.wait_ge(sem("uq_copied"), 3)
                for u in (u0, u0 + 1):
                    start_unit(u)
                    kt = u - u0
                    a = tiles(o_hi, kt, kt + 1), tiles(o_lo, kt, kt + 1)
                    for h in range(4):
                        feature_product(bank[5 + h // 2][:, (h % 2) * S:(h % 2 + 1) * S], u,
                                        lambda r: r[:, h * P:(h + 1) * P], *a, kt == 0 and h % 2 == 0, kt == 1)
                    for r2 in range(2):
                        ins = feature_product(
                            bank[7][:, r2 * S:(r2 + 1) * S], u,
                            lambda r: r[:, (4 + r2) * P:(5 + r2) * P],
                            *a, kt == 0 and r2 == 0, kt == 1)
                    if kt == 0:
                        ins.then_inc(sem("w_used"), 1)
                end_chunk(ins)
                pe.wait_ge(sem("uq_copied"), 3 * j + 3)
                pe.wait_ge(sem("c_rooted"), 2)
                if j:
                    pe.wait_ge(sem("q_rotated"), 1)
                for i in range(2):
                    ins = pe.matmul(bank[3][:, i * S:(i + 1) * S], const(C_SWAP32, P), tiles(of, 4 + i, 5 + i),
                                    start=True, stop=True)
                ins.then_inc(sem("q_swapped"), 1)
                u0 = unit0("ukv", j)
                pe.wait_ge(sem("kr_ready"), 1)
                if j:
                    pe.wait_ge(sem("ukv_copied"), 4)
                for u in (u0, u0 + 1):
                    start_unit(u)
                    kt = u - u0
                    a = tiles(o_hi, 2 + kt, 3 + kt), tiles(o_lo, 2 + kt, 3 + kt)
                    for h in range(4):
                        feature_product(bank[h // 2][:, (h % 2) * S:(h % 2 + 1) * S], u,
                                        lambda r: r[:, h * 256:h * 256 + P], *a, kt == 0 and h % 2 == 0, kt == 1)
                    for t in range(2):
                        ins = token_product(
                            bank[2 + 2 * t][:, :], u,
                            lambda r: r.rearrange("p (h c) -> p h c", h=4)[:, :, NOPE:256],
                            a[0][:, t * P:(t + 1) * P], a[1][:, t * P:(t + 1) * P], kt == 0, kt == 1)
                    if kt == 0:
                        ins.then_inc(sem("w_used"), 1)
                end_chunk(ins)
            pe.wait_ge(sem("uq_copied"), 6)
            pe.wait_ge(sem("ukv_copied"), 8)
            pe.wait_ge(sem("q_rotated"), 2)
            attention("mla",
                      lambda h: [(tiles(qz, h, h + 1), tiles(kk, h, h + 1)),
                                 (tiles(of, h // 2, h // 2 + 1), tiles(of, 6 + h % 2, 7 + h % 2))],
                      lambda h, t: vtile(t, h), False)
            pe.wait_ge(sem("shifted"), 8)
            fold(1, (0, 1))
            out_projection("mla_o", 2)
            norm_sums(0)
            ffn(0)
            norm_sums(1)

            for i in range(8):
                end_chunk(columns_chunk(("moba_in", i), turn(("moba_in", i)), (h_hi, h_lo), e=None if i else 2))
                if i >= 6:
                    fold(5, (5, 6), (0, 1) if i == 6 else (2, 3))

            def token_chunk(key):
                b = turn(key)
                u0 = unit0(*key)
                for u in (u0, u0 + 1):
                    start_unit(u)
                    for k in range(4):
                        kt = 4 * (u - u0) + k
                        for t in range(2):
                            at = kt * S + t * P
                            ins = token_product(b[:, t * S:(t + 1) * S], u, lambda r: r[:, k * 256:(k + 1) * 256],
                                                h_hi[:, at:at + P], h_lo[:, at:at + P], kt == 0 and t == 0,
                                                kt == KT - 1)
                    if u == u0:
                        ins.then_inc(sem("w_used"), 1)
                end_chunk(ins)

            for i in range(8, 12):
                token_chunk(("moba_in", i))
            pe.wait_ge(sem("turn_read"), 12)
            attention("moba", lambda h: [(tiles(qz, h, h + 1), tiles(kk, h, h + 1))],
                      lambda h, t: vtile(t, h), False)
            pe.wait_ge(sem("shifted"), 16)
            out_projection("moba_o", 6)
            norm_sums(2)
            ffn(1)
            norm_sums(3)
            norm_sums(4, False)

            key = ("a_kv", 0)
            end_chunk(columns_chunk(key, turn(key), (h_hi, h_lo), e=4))
            key = ("f", 0)
            end_chunk(columns_chunk(key, turn(key), (h_hi, h_lo), 16))
            fold(8, (5, 6))
            for name in ("a_q", "b_q"):
                for m in range(2):
                    end_chunk(columns_chunk((name, m), turn((name, m)), (h_hi, h_lo)))
            pe.wait_ge(sem("turn_read"), turn_of[("a_kv", 0)] + 1)
            pe.matmul(bank[4][:, 0:S], const(C_SWAP64, P), tiles(kk, 8, 9), start=True, stop=True)
            for t in range(2):
                ins = pe.transpose(bank[4][:, S + t * P:S + (t + 1) * P], tiles(kk, 9, 10)[:, t * P:(t + 1) * P],
                                   ident)
            ins.then_inc(sem("akv_turned"), 1)
            for m in range(2):
                end_chunk(columns_chunk(("b_k", m), turn(("b_k", m)), (h_hi, h_lo)))
            for m in range(2):
                token_chunk(("b_v", m))
            pe.wait_ge(sem("turn_read"), turn_of[("b_v", 1)] + 1)
            pe.wait_ge(sem("akv_spread"), 8)
            attention("swa",
                      lambda h: [(tiles(qz, h // 2, h // 2 + 1), tiles(kk, h // 4 * 2 + h % 2, h // 4 * 2 + h % 2 + 1))],
                      lambda h, t: vtile(t, h // 4 * 2 + h % 2), True)
            pe.wait_ge(sem("decay_ready"), 9)
            pe.wait_ge(sem("shifted"), 24)
            pe.wait_ge(sem("probT_ready"), 24)
            pe.wait_ge(sem("pair_read"), 4)
            attention("fgt",
                      lambda h: [(tiles(qz, 4 + h // 2, 5 + h // 2), tiles(kk, 4 + h, 5 + h)),
                                 (rstd[:, S:2 * S], tiles(bias, h, h + 1))],
                      lambda h, t: vtile(t, 4 + h), True)
            pe.wait_ge(sem("shifted"), 32)
            for m in range(4):
                key = ("a_gate", m)
                end_chunk(columns_chunk(key, turn(key), (h_hi, h_lo)))
            out_projection("attn_o", 9)
            norm_sums(5, False)

            for m in range(4):
                key = ("xr", m)
                end_chunk(columns_chunk(key, turn(key), (h_hi, h_lo), e=None if m else 5))
            for m in range(LRU_EARLY):
                key = ("l_gate", m)
                end_chunk(columns_chunk(key, turn(key), (h_hi, h_lo)))
            pe.wait_ge(sem("turn_read"), turn_of[("l_gate", LRU_EARLY - 1)] + 1)
            pe.wait_ge(sem("z_ready"), 40)
            for i, name in enumerate(("w_a", "w_x")):
                u0 = unit0(name, 0)
                for u in (u0, u0 + 1):
                    start_unit(u)
                    for k in range(4):
                        n = 4 * (u - u0) + k
                        if i == 0:
                            pe.wait_ge(sem("xc_ready"), n // 2 + 1)
                        ins = feature_product(bank[4 * i + n // 2][:, (n % 2) * S:(n % 2 + 1) * S], u,
                                              lambda r: r[:, k * P:(k + 1) * P], tiles(o_hi, n, n + 1),
                                              tiles(o_lo, n, n + 1), True, True)
                    ins.then_inc(sem("w_used"), 1)
            pe.wait_ge(sem("rg_read"), 8)
            for m in range(LRU_EARLY, 4):
                key = ("l_gate", m)
                end_chunk(columns_chunk(key, turn(key), (h_hi, h_lo)))
            pe.wait_ge(sem("rg_read"), 16)
            out_projection("lru_o")
            norm_sums(6, False)
            for t in range(2):
                for m in range(KT):
                    pe.wait_ge(sem("h_full"), 8 * 6 + m + 1)
                    b = bank[4 + 2 * t + m // 4]
                    ins = pe.transpose(b[:, (m % 4) * P:(m % 4 + 1) * P], qz[:, m * S + t * P:m * S + (t + 1) * P],
                                       ident)
                    if m % 4 == 3:
                        ins.then_inc(sem("y_turned"), 1)

        @block.scalar
        def _(act):
            nxt = [0]

            def ahead(u):
                while nxt[0] <= min(u, NU - 1):
                    v = nxt[0]
                    if v % 2 == 0:
                        act.wait_ge(sem(f"w_in{v // 2 % RAW}"), landed[v // 2])
                    if v >= UNITS:
                        act.wait_ge(sem("w_used"), v - UNITS + 1)
                    act.activation(hi(v), raw_unit(v), ACT.Copy).then_inc(sem("w_hi_ready"), 1)
                    nxt[0] += 1

            def product(*key):
                u = unit0(*key) + 1
                ahead(u + AHEAD)
                act.wait_ge(sem("w_used"), u + 1)

            def h_high(e, m, src):
                act.activation(tiles(h_hi, m, m + 1), tiles(src, m, m + 1), ACT.Identity,
                               bias=lncol[:, 16 * e + 8 + m:16 * e + 9 + m],
                               scale=lncol[:, 16 * e + m:16 * e + m + 1]).then_inc(sem("h_hi_ready"), 1)

            def norm(n, e, eps):
                for m in range(KT):
                    if n < 4:
                        act.wait_ge(sem("centered"), 8 * n + m + 1)
                    elif n == 4:
                        act.wait_ge(sem("x_ready"), 24 + m + 1)
                    else:
                        act.wait_ge(sem("z_ready"), 8 * (n - 1) + m + 1)
                    if n != 4:
                        act.activation(tiles(kk, m, m + 1), tiles(qz if n < 4 else x, m, m + 1),
                                       ACT.Square).then_inc(sem("squared"), 1)
                act.wait_ge(sem("var_done"), n + 1)
                act.activation(rstd[:, 0:S], bank[2][:, 0:S], ACT.Sqrt, bias=eps, scale=1.0 / D).then_inc(
                    sem("rooted"), 1)
                if e is None and n != 3:
                    return
                for m in range(KT):
                    act.wait_ge(sem("normed"), 8 * n + m + 1)
                    if e is not None:
                        h_high(e, m, qz)
                    if n < 4:
                        act.activation(tiles(x, m, m + 1), tiles(qz, m, m + 1), ACT.Identity,
                                       bias=pcol["ln_b"][:, 8 * n + m:8 * n + m + 1],
                                       scale=pcol["ln_g"][:, 8 * n + m:8 * n + m + 1]).then_inc(sem("x_ready"), 1)

            def attention(kind, pair, first_unit):
                h0 = HEAD[kind]
                ahead(first_unit + AHEAD)
                sc = SCALE[kind]
                for t in range(HEADS + 3):
                    if t < HEADS:
                        g = h0 + t
                        p = head_cols(prob, g % SD)
                        st = stat[:, (g % SD) * 12:(g % SD + 1) * 12]
                        act.wait_ge(sem("shifted"), g + 1)
                        act.activation(p[:, 0:P], p[:, 0:P], ACT.Exp, bias=st[:, 2:3], scale=sc,
                                       accum_out=st[:, 4:5]).then_inc(sem("exped"), 1)
                        act.activation(p[:, P:CAUSAL], p[:, P:CAUSAL], ACT.Exp, bias=st[:, 3:4], scale=sc,
                                       accum_out=st[:, 5:6]).then_inc(sem("exped"), 1)
                        if kind == "swa":
                            act.activation(st[:, 8:10], st[:, 2:4], ACT.Exp,
                                           bias=sinks[:, t:t + 1]).then_inc(sem("sink_ready"), 1)
                    if 1 <= t < HEADS + 1:
                        g = h0 + t - 1
                        p = head_cols(prob, g % SD)
                        st = stat[:, (g % SD) * 12:(g % SD + 1) * 12]
                        act.wait_ge(sem("inverse_ready"), g + 1)
                        act.activation(p[:, 0:P], p[:, 0:P], ACT.Copy, scale=st[:, 6:7]).then_inc(
                            sem("prob_part"), 1)
                        act.activation(p[:, P:CAUSAL], p[:, P:CAUSAL], ACT.Copy, scale=st[:, 7:8]).then_inc(
                            sem("prob_ready"), 1)
                    if 2 <= t < HEADS + 2:
                        g = h0 + t - 2
                        act.wait_ge(sem("prob_turned"), g + 1)
                        if g >= 2:
                            act.wait_ge(sem("head_out"), g - 1)
                        elif g == 0:
                            act.wait_ge(sem("ebias_out"), 16)
                        act.activation(head_cols(probT, g % 2), bank[2 + t % 2][:, 0:CAUSAL],
                                       ACT.Copy).then_inc(sem("probT_ready"), 1)
                    if t >= 3:
                        h = t - 3
                        if not pair:
                            act.wait_ge(sem("head_out"), h0 + h + 1)
                            act.activation(tiles(o_hi, h, h + 1), bank[(4, 7)[h % 2]][:, 0:S],
                                           ACT.Copy).then_inc(sem("o_hi_ready"), 1)
                        elif h % 2:
                            act.wait_ge(sem("head_out"), h0 + h + 1)
                            n = h // 2 + (4 if kind == "fgt" else 0)
                            act.activation(tiles(of, n, n + 1), bank[(4, 7)[h // 2 % 2]][:, 0:S],
                                           ACT.Copy).then_inc(sem("pair_read"), 1)

            def ffn(l):
                w2, cb = pcol[f"conv_w{l}"], pcol[f"conv_b{l}"]
                for i in range(FI):
                    n = l * FI + i
                    product("ffa", l, i)
                    for t in range(2):
                        f = 2 * i + t
                        s = 2 * (n % 2) + t
                        act.activation(tiles(conv, s, s + 1), bank[0][:, t * S:(t + 1) * S], ACT.Identity,
                                       bias=cb[:, f:f + 1], scale=w2[:, 2 * FT + f:2 * FT + f + 1]).then_inc(
                                           sem("ff_c0"), 1)
                    s = 2 * (n % 2)
                    act.wait_ge(sem("ff_conv"), 2 * n + 2)
                    act.activation(tiles(gated, s, s + 2), tiles(conv, s, s + 2), ACT.Gelu_apprx_tanh).then_inc(
                        sem("ff_gelu"), 1)
                    product("ffb", l, i)
                    act.wait_ge(sem("ff_gated"), n + 1)
                    act.activation(tiles(o_hi, s, s + 2), tiles(gated, s, s + 2), ACT.Copy).then_inc(
                        sem("ff_g_hi"), 1)
                product("ffo", l, FI - 1)

            act.wait_ge(sem("c_turned"), 1)
            act.activation(c_act, bank[3][:, 0:16], ACT.Silu).then_inc(sem("c_act"), 1)
            srcs = {
                "c": w["c"], "c_2": w["c_2"], "q_norm": w["mla_q_norm"], "kv_norm": w["mla_kv_norm"],
                "norm_g": w["norm_g_2"], "final_g": w["final_g_2"], "conv2_w": w["lru_conv_w_2"],
                "conv2_b": w["lru_conv_b_2"], "b_a": w["lru_b_a_2"], "b_x": w["lru_b_x_2"],
                "lam": w["lru_lambda_2"], "mod_b": w["mod_b"], "ada_b": w["ada_b_2"], "ln_g": w["ln_g"],
                "ln_b": w["ln_b"], "conv_w0": w["ffn_conv_w"][0], "conv_b0": w["ffn_conv_b"][0:1],
                "conv_w1": w["ffn_conv_w"][1], "conv_b1": w["ffn_conv_b"][1:2],
            }
            for b, rows in enumerate(PB):
                at = 0
                for name, n in rows:
                    s = srcs[name]
                    if name in ("c", "c_2"):
                        at += n
                        continue
                    names = " ".join("abc"[:len(s.shape)])
                    if len(s.shape) > 1:
                        s = s.rearrange(f"{names} -> ({names})")
                    act.dma_start(prow[at:at + n, b * P:(b + 1) * P],
                                 s.rearrange("(n q) -> n q", q=P)).then_inc(sem("params_in"), 16)
                    at += n
            act.wait_ge(sem("params_turned"), 1)
            for b, rows in enumerate(PB):
                n = sum(r[1] for r in rows)
                act.activation(cols[:, b * P:b * P + n], bank[b // 4][:, (b % 4) * P:(b % 4) * P + n],
                               ACT.Copy).then_inc(sem("cols_ready"), 1)
            for m in range(4):
                act.wait_ge(sem("x_turned"), 2 * m + 2)
                act.activation(tiles(x, 2 * m, 2 * m + 2), bank[4 + m][:, :], ACT.Copy).then_inc(sem("x_copied"), 1)
            act.wait_ge(sem("bias_turned"), 1)
            act.activation(probT[0:8, 0:2 * S], bank[3][0:8, :], ACT.Copy, scale=1 / SCALE["swa"]).then_inc(
                sem("bias_row"), 1)
            ahead(AHEAD)
            for m in range(KT):
                act.wait_ge(sem("h_full"), m + 1)
                h_high(0, m, x)

            for j in range(2):
                product("mla_in", j)
                act.activation(tiles(kk, 2 * j, 2 * j + 2), bank[j][:, :], ACT.Square).then_inc(sem("c_squared"), 1)
            for j in range(2):
                if j:
                    product("mla_in", 2)
                    act.activation(tiles(kk, 4, 5)[0:64, :], bank[2][0:64, 0:S], ACT.Copy).then_inc(
                        sem("kr_copied"), 1)
                act.wait_ge(sem("c_summed"), j + 1)
                act.activation(tiles(rstd, j, j + 1), bank[3][:, j * S:(j + 1) * S], ACT.Sqrt, bias=RMS_EPS,
                               scale=1.0 / MLA_RANK).then_inc(sem("c_rooted"), 1)
            for j in range(2):
                act.wait_ge(sem("c_full"), 2 * j + 2)
                act.activation(tiles(o_hi, 2 * j, 2 * j + 2), tiles(hf, 2 * j, 2 * j + 2), ACT.Copy).then_inc(
                    sem("c_hi"), 1)
            act.wait_ge(sem("turned_angles"), 2)
            act.activation(cos, cos, ACT.Sin).then_inc(sem("rotary"), 1)
            act.activation(sin, sin, ACT.Sin, scale=const(C_COL + 1)).then_inc(sem("rotary"), 1)
            for j in range(2):
                product("uq", j)
                act.activation(tiles(qz, 4 * j, 4 * j + 2), bank[5][:, :], ACT.Copy).then_inc(sem("uq_copied"), 1)
                act.activation(tiles(qz, 4 * j + 2, 4 * j + 4), bank[6][:, :], ACT.Copy).then_inc(sem("uq_copied"), 1)
                if j:
                    act.wait_ge(sem("q_rotated"), 1)
                act.activation(tiles(of, 4, 6), bank[7][:, :], ACT.Copy).then_inc(sem("uq_copied"), 1)
                product("ukv", j)
                if j:
                    act.wait_ge(sem("kr_ready"), 1)
                for i in range(2):
                    act.activation(tiles(kk, 4 * j + 2 * i, 4 * j + 2 * i + 2), bank[i][:, :], ACT.Copy).then_inc(
                        sem("ukv_copied"), 1)
                for t in range(2):
                    at = (t * 12 + 4 * j) * P
                    act.activation(vv[:, at:at + 4 * P], bank[2 + 2 * t][:, :], ACT.Copy).then_inc(
                        sem("ukv_copied"), 1)
            attention("mla", False, unit0("mla_o", 0))
            for m in range(4):
                product("mla_o", m)
            norm(0, 1, LN_EPS / ALPHA ** 2)
            ffn(0)
            norm(1, 2, LN_EPS / ALPHA ** 2)

            def turned(key):
                product(*key)
                return bank[turn_of[key] % 4]

            for i in range(8):
                b = turned(("moba_in", i))
                dst = qz if i < 4 else kk
                act.activation(tiles(dst, 2 * (i % 4), 2 * (i % 4) + 2), b[:, :], ACT.Copy).then_inc(
                    sem("turn_read"), 1)
            for i in range(4):
                b = turned(("moba_in", 8 + i))
                dst = vv[:, :].rearrange("p (t f) -> p t f", t=2)[:, :, 2 * i * P:(2 * i + 2) * P]
                act.activation(dst, grid(b[:, :], 2), ACT.Copy).then_inc(sem("turn_read"), 1)
            attention("moba", False, unit0("moba_o", 0))
            for m in range(4):
                product("moba_o", m)
            norm(2, 3, LN_EPS / ALPHA ** 2)
            ffn(1)
            norm(3, None, LN_EPS / ALPHA ** 2)
            norm(4, 4, RMS_EPS)

            b = turned(("a_kv", 0))
            act.activation(tiles(kk, 8, 10), b[:, :], ACT.Copy).then_inc(sem("turn_read"), 1)
            b = turned(("f", 0))
            act.wait_ge(sem("attn_in"), 16 * 3)
            act.activation(prob[0:16, 0:S], b[0:16, 0:S], ACT.Identity, bias=bf[:, :]).then_inc(sem("turn_read"), 1)
            for i, name in enumerate(("a_q", "b_q")):
                for m in range(2):
                    b = turned((name, m))
                    at = 4 * i + 2 * m
                    act.activation(tiles(qz, at, at + 2), b[:, :], ACT.Copy).then_inc(sem("turn_read"), 1)
            act.wait_ge(sem("f_abs"), 1)
            act.activation(prob[0:16, 2 * S:3 * S], prob[0:16, S:2 * S], ACT.Exp, scale=-1.0).then_inc(
                sem("f_exp"), 1)
            act.wait_ge(sem("akv_turned"), 1)
            act.wait_ge(sem("akv_spread"), 8)
            for m in range(2):
                b = turned(("b_k", m))
                dst = grid(kk[:, (4 + 4 * m) * S:(8 + 4 * m) * S], 2)
                act.activation(dst[:, :, 0:S], grid(b[:, :], 2), ACT.Copy, scale=half[0]).then_inc(
                    sem("bk_low"), 1)
                act.activation(dst[:, :, S:2 * S], grid(b[:, :], 2), ACT.Copy, scale=half[1]).then_inc(
                    sem("turn_read"), 1)
            act.wait_ge(sem("vv_zero"), 1)
            for m in range(2):
                b = turned(("b_v", m))
                for o in range(2):
                    src = b[:, :].rearrange("p (t i o f) -> p t i o f", t=2, i=2, o=2)[:, :, :, o, :]
                    dst = vv[:, :].rearrange("p (t i o f) -> p t i o f", t=2, i=6, o=2)
                    dst = dst[:, :, 2 + 2 * m:4 + 2 * m, o, o * 64:(o + 1) * 64]
                    for t in range(2):
                        last = act.activation(dst[:, t], src[:, t], ACT.Copy)
                        last.then_inc(sem("turn_read" if o and t else "bv_part"), 1)
            attention("swa", True, unit0("a_gate", 0))
            act.wait_ge(sem("lam_abs"), 1)
            act.activation(small[:, 48:56], small[:, 40:48], ACT.Exp, scale=-1.0).then_inc(
                sem("lam_exp"), 1)
            attention("fgt", True, unit0("a_gate", 0))
            for m in range(4):
                b = turned(("a_gate", m))
                if m >= 2:
                    act.wait_ge(sem("head_gated"), m - 1)
                act.activation(prob[:, (m % 2) * 512:(m % 2 + 1) * 512], b[:, :], ACT.Silu).then_inc(
                    sem("turn_read"), 1)
                act.wait_ge(sem("head_gated"), m + 1)
                act.activation(tiles(o_hi, 2 * m, 2 * m + 2), tiles(of, 2 * m, 2 * m + 2), ACT.Copy).then_inc(
                    sem("o_hi_ready"), 1)
            for m in range(4):
                product("attn_o", m)
            norm(5, 5, RMS_EPS)

            for m in range(4):
                b = turned(("xr", m))
                for t in range(2):
                    f = 2 * m + t
                    act.activation(tiles(kk, f, f + 1), b[:, t * S:(t + 1) * S], ACT.Identity,
                                   bias=pcol["conv2_b"][:, f:f + 1],
                                   scale=pcol["conv2_w"][:, 24 + f:25 + f]).then_inc(sem("xc_started"), 1)
                act.wait_ge(sem("xc_full"), 2 * m + 2)
                act.activation(tiles(o_hi, 2 * m, 2 * m + 2), tiles(kk, 2 * m, 2 * m + 2), ACT.Copy).then_inc(
                    sem("xc_hi"), 1)
            for m in range(LRU_EARLY):
                b = turned(("l_gate", m))
                act.activation(prob[:, m * 512:(m + 1) * 512], b[:, :], ACT.Silu).then_inc(sem("turn_read"), 1)
            for i, (name, dst, pb) in enumerate((("w_a", qz, "b_a"), ("w_x", vv, "b_x"))):
                product(name, 0)
                for n in range(KT):
                    act.activation(tiles(dst, n, n + 1), bank[4 * i + n // 2][:, (n % 2) * S:(n % 2 + 1) * S],
                                   ACT.Sigmoid, bias=pcol[pb][:, n:n + 1]).then_inc(sem("rg_read"), 1)
            ahead(unit0("l_gate", LRU_EARLY) + AHEAD)
            for i in range(2):
                act.wait_ge(sem("rate_ready"), 4 * i + 4)
                act.activation(tiles(bias, 4 * i, 4 * i + 4), tiles(qz, 4 * i, 4 * i + 4), ACT.Tanh).then_inc(
                    sem("rate_tanh"), 1)
                act.wait_ge(sem("rate_tanh"), i + 1)
                act.activation(tiles(of, 4 * i, 4 * i + 4), tiles(qz, 4 * i, 4 * i + 4), ACT.Exp,
                               scale=2.0).then_inc(sem("decay_exp"), 1)
                act.wait_ge(sem("decay_exp"), 2 * i + 1)
                act.activation(tiles(qz, 4 * i, 4 * i + 4), tiles(qz, 4 * i, 4 * i + 4), ACT.Exp).then_inc(
                    sem("decay_exp"), 1)
            ahead(unit0("l_gate", LRU_EARLY) + 1 + AHEAD)
            for i in range(2):
                act.wait_ge(sem("ratio_ready"), i + 1)
                act.activation(tiles(of, 4 * i, 4 * i + 4), tiles(of, 4 * i, 4 * i + 4), ACT.Sqrt,
                               scale=-1.0).then_inc(sem("input_root"), 1)
            for m in range(LRU_EARLY, 4):
                b = turned(("l_gate", m))
                act.wait_ge(sem("ix_ready"), 2)
                act.activation(tiles(kk, 2 * m, 2 * m + 2), b[:, :], ACT.Silu).then_inc(sem("turn_read"), 1)
            for m in range(4):
                act.wait_ge(sem("l_gated"), m + 1)
                act.activation(tiles(o_hi, 2 * m, 2 * m + 2), tiles(kk, 2 * m, 2 * m + 2), ACT.Copy).then_inc(
                    sem("o_hi_ready"), 1)
            for m in range(4):
                product("lru_o", m)
            norm(6, None, RMS_EPS)
            for t in range(2):
                for i in range(2):
                    act.wait_ge(sem("y_turned"), 2 * t + i + 1)
                    at = t * D + i * 512
                    act.activation(kk[:, at:at + 512], bank[4 + 2 * t + i][:, :], ACT.Copy).then_inc(
                        sem("out_rows"), 1)

        @block.vector
        def _(dve):
            nxt, mod_n, fold_n, chain = [0], [0], [0], [0]

            def link(ins):
                chain[0] += 1
                ins.then_inc(sem("vec_step"), 1)
                dve.wait_ge(sem("vec_step"), chain[0])

            def magnitude(dst, src):
                return dve.scalar_tensor_tensor(dst, src, -1.0, src, ALU.mult, ALU.max)

            def ahead(u):
                while nxt[0] <= min(u, NU - 1):
                    v = nxt[0]
                    dve.wait_ge(sem("w_hi_ready"), v + 1)
                    dve.tensor_tensor(lo(v), raw_unit(v), hi(v).bitcast(F32), ALU.subtract).then_inc(
                        sem("w_lo_ready"), 1)
                    nxt[0] += 1

            def product(*key):
                u = unit0(*key) + 1
                ahead(u + AHEAD)
                dve.wait_ge(sem("w_used"), u + 1)

            last_sum = {1: 0, 4: 1, 5: 3, 6: 4, 7: 5, 8: 6, 9: 8}

            def modulate(count):
                for n in range(mod_n[0], mod_n[0] + count):
                    g, k, _ = mods[n]
                    width = mod_width[g]
                    acc = modacc[g][:, 0:width]
                    ck = c_act[:, (8 if g >= 7 else 0) + k:(8 if g >= 7 else 0) + k + 1]
                    slot = mod_slot[n]
                    src = early_slot(n) if n in early else modraw[:, slot, 0:width]
                    dve.wait_ge(sem(f"mod_early{n}" if n in early else f"mod_in{slot}"), mod_landed[n])
                    if k == 0:
                        if g in last_sum:
                            dve.wait_ge(sem("fold_turned"), parts_before[last_sum[g] + 1])
                        ins = dve.tensor_scalar(acc, src, ck, None, ALU.mult)
                    else:
                        dve.wait_ge(sem("mod_summed"), n)
                        ins = dve.scalar_tensor_tensor(acc, src, ck, acc, ALU.mult, ALU.add)
                    ins.then_inc(sem("mod_summed"), 1)
                mod_n[0] += count

            def fold(g, b, parts=range(4)):
                for part in parts[:mod_width[g] // (4 * P)]:
                    n = fold_n[0]
                    dve.wait_ge(sem("fold_turned"), n + 1)
                    at = 16 * g + 4 * part
                    dve.tensor_reduce(modc[:, at:at + 4],
                                      bank[b[n % 2]][:, :].rearrange("p (i c) -> p i c", i=4),
                                      AX.X, ALU.add).then_inc(sem("fold_summed"), 1)
                    fold_n[0] += 1
                if fold_n[0] < parts_before[g] + mod_width[g] // (4 * P):
                    return
                dve.wait_ge(sem("fold_summed"), fold_n[0])
                biases = {0: [("mod_b", 0, 16)], 1: [("mod_b", 16, 16)], 2: [("mod_b", 32, 8)],
                          3: [("mod_b", 40, 8)], 4: [("mod_b", 48, 16)], 5: [("mod_b", 64, 16)],
                          6: [("mod_b", 80, 16)], 7: [("ada_b", 0, 16)],
                          8: [("ada_b", 16, 8), ("ada_b", 40, 8)], 9: [("ada_b", 24, 16)]}
                at = 16 * g
                for name, r, n in biases[g]:
                    link(dve.tensor_tensor(modc[:, at:at + n], modc[:, at:at + n], pcol[name][:, r:r + n],
                                           ALU.add))
                    at += n

            def mod8(g, half):
                return modc[:, 16 * g + 8 * half:16 * g + 8 * half + 8]

            def coefficients(e, shift, scale, gain=None, offset=None):
                cs, ct = lncol[:, 16 * e:16 * e + 8], lncol[:, 16 * e + 8:16 * e + 16]
                link(dve.tensor_scalar(cs, scale, 1.0, None, ALU.add))
                if offset is not None:
                    link(dve.tensor_tensor(ct, offset, cs, ALU.mult))
                    link(dve.tensor_tensor(ct, ct, shift, ALU.add))
                else:
                    link(dve.tensor_copy(ct, shift))
                if gain is not None:
                    link(dve.tensor_tensor(cs, cs, gain, ALU.mult))

            def gate(r, src, scale):
                link(dve.tensor_scalar(gates[:, 8 * r:8 * r + 8], src, scale, None, ALU.mult))

            def h_full(e, m, src):
                dve.tensor_scalar(tiles(hf, m % 4, m % 4 + 1), src, lncol[:, 16 * e + m:16 * e + m + 1],
                                  lncol[:, 16 * e + 8 + m:16 * e + 9 + m], ALU.mult, ALU.add).then_inc(
                                      sem("h_full"), 1)

            def h_low(e, m):
                dve.wait_ge(sem("h_full"), 8 * e + m + 1)
                dve.wait_ge(sem("h_hi_ready"), 8 * e + m + 1)
                dve.tensor_tensor(tiles(h_lo, m, m + 1), tiles(hf, m % 4, m % 4 + 1),
                                  tiles(h_hi, m, m + 1).bitcast(F32), ALU.subtract).then_inc(sem("h_ready"), 1)

            def residual(r, m, y):
                dve.scalar_tensor_tensor(tiles(qz if r < 4 else x, m, m + 1), y, gates[:, 8 * r + m:8 * r + m + 1],
                                         tiles(x, m, m + 1), ALU.mult, ALU.add).then_inc(sem("z_ready"), 1)

            def out_projection(name, r, after=lambda i: None):
                for i in range(4):
                    product(name, i)
                    for t in range(2):
                        residual(r, 2 * i + t, bank[5 + i % 2][:, t * S:(t + 1) * S])
                    after(i)

            def norm(n, e):
                if n < 4:
                    dve.wait_ge(sem("mean_done"), n + 1)
                    for m in range(KT):
                        dve.scalar_tensor_tensor(tiles(qz, m, m + 1), bank[3][:, 0:S], -1.0 / D,
                                                 tiles(qz, m, m + 1), ALU.mult, ALU.add).then_inc(
                                                     sem("centered"), 1)
                if n == 4:
                    for m in range(KT):
                        dve.wait_ge(sem("x_ready"), 24 + m + 1)
                        dve.tensor_tensor(tiles(kk, m, m + 1), tiles(x, m, m + 1), tiles(x, m, m + 1),
                                          ALU.mult).then_inc(sem("squared"), 1)
                dve.wait_ge(sem("rooted"), n + 1)
                link(dve.reciprocal(tiles(rstd, 1, 2), tiles(rstd, 0, 1)))
                for m in range(KT + 2):
                    if m < KT:
                        dve.tensor_tensor(tiles(qz, m, m + 1), tiles(qz if n < 4 else x, m, m + 1),
                                          tiles(rstd, 1, 2), ALU.mult).then_inc(sem("normed"), 1)
                    if 1 <= m <= KT and (e is not None or n == 6):
                        dve.wait_ge(sem("normed"), 8 * n + m)
                        if n == 6:
                            f = pcol["final_g"][:, m - 1:m]
                            dve.tensor_scalar(tiles(qz, m - 1, m), tiles(qz, m - 1, m), f, None,
                                              ALU.mult).then_inc(sem("h_full"), 1)
                        else:
                            h_full(e, m - 1, tiles(qz, m - 1, m))
                    if m >= 2 and e is not None:
                        h_low(e, m - 2)

            def attention(kind, pair, first_unit, mod_steps, bias_of):
                h0 = HEAD[kind]
                ahead(first_unit + AHEAD)
                for t in range(HEADS + 4):
                    if t < HEADS:
                        g = h0 + t
                        p = head_cols(prob, g % SD)
                        st = stat[:, (g % SD) * 12:(g % SD + 1) * 12]
                        dve.wait_ge(sem("scores"), g + 1)
                        if g >= SD:
                            dve.wait_ge(sem("prob_turned"), g - SD + 1)
                        if kind == "moba":
                            dve.wait_ge(sem("alibi"), t + 1)
                        own, both = bias_of(t)
                        b = bank[t % 2]
                        dve.tensor_tensor_reduce(p[:, 0:P], b[:, 0:P], own, 1.0, NEG, ALU.add, ALU.max,
                                                 st[:, 0:1]).then_inc(sem("row_max"), 1)
                        dve.tensor_tensor_reduce(p[:, P:CAUSAL], b[:, P:CAUSAL], both, 1.0, NEG, ALU.add, ALU.max,
                                                 st[:, 1:2]).then_inc(sem("row_max"), 1)
                        dve.wait_ge(sem("row_max"), 2 * g + 2)
                        if kind == "swa":
                            link(dve.tensor_scalar(st[:, 10:12], st[:, 0:2], SCALE[kind], sinks[:, t:t + 1],
                                                   ALU.mult, ALU.max))
                            dve.tensor_scalar(st[:, 2:4], st[:, 10:12], -1.0, None, ALU.mult).then_inc(
                                sem("shifted"), 1)
                        else:
                            dve.tensor_scalar(st[:, 2:4], st[:, 0:2], -SCALE[kind], None, ALU.mult).then_inc(
                                sem("shifted"), 1)
                    if 1 <= t < HEADS + 1:
                        g = h0 + t - 1
                        st = stat[:, (g % SD) * 12:(g % SD + 1) * 12]
                        dve.wait_ge(sem("exped"), 2 * g + 2)
                        if kind == "swa":
                            dve.wait_ge(sem("sink_ready"), t)
                            link(dve.tensor_tensor(st[:, 4:6], st[:, 4:6], st[:, 8:10], ALU.add))
                        dve.reciprocal(st[:, 6:8], st[:, 4:6]).then_inc(sem("inverse_ready"), 1)
                    if t >= 4 and not pair:
                        h = t - 4
                        dve.wait_ge(sem("o_hi_ready"), h0 + h + 1)
                        dve.tensor_tensor(tiles(o_lo, h, h + 1), bank[(4, 7)[h % 2]][:, 0:S],
                                          tiles(o_hi, h, h + 1).bitcast(F32), ALU.subtract).then_inc(
                                              sem("o_ready"), 1)
                    if t in mod_steps:
                        modulate(1)

            def ffn(l):
                w01 = pcol[f"conv_w{l}"]
                for i in range(FI):
                    n = l * FI + i
                    s = 2 * (n % 2)
                    product("ffa", l, i)
                    for t in range(2):
                        f = 2 * i + t
                        dve.wait_ge(sem("ff_c0"), 2 * n + 2)
                        c, a = tiles(conv, s + t, s + t + 1), bank[0][:, t * S:(t + 1) * S]
                        dve.scalar_tensor_tensor(c[:, 1:S], a[:, 0:S - 1], w01[:, FT + f:FT + f + 1], c[:, 1:S],
                                                 ALU.mult, ALU.add).then_inc(sem("ff_tap"), 1)
                    for t in range(2):
                        f = 2 * i + t
                        dve.wait_ge(sem("ff_tap"), 2 * n + t + 1)
                        c, a = tiles(conv, s + t, s + t + 1), bank[0][:, t * S:(t + 1) * S]
                        dve.scalar_tensor_tensor(c[:, 2:S], a[:, 0:S - 2], w01[:, f:f + 1], c[:, 2:S],
                                                 ALU.mult, ALU.add).then_inc(sem("ff_conv"), 1)
                    product("ffb", l, i)
                    dve.wait_ge(sem("ff_gelu"), n + 1)
                    dve.tensor_tensor(tiles(gated, s, s + 2), tiles(gated, s, s + 2), bank[1][:, :],
                                      ALU.mult).then_inc(sem("ff_gated"), 1)
                    dve.wait_ge(sem("ff_g_hi"), n + 1)
                    dve.tensor_tensor(tiles(o_lo, s, s + 2), tiles(gated, s, s + 2),
                                      tiles(o_hi, s, s + 2).bitcast(F32), ALU.subtract).then_inc(
                                          sem("ff_g_ready"), 1)
                    if i >= FI - 2:
                        fold((4, 7)[l], (2, 3), (0, 1) if i == FI - 2 else (2, 3))
                    if l == 0 and i == FI - 3:
                        fold(3, (2, 3))
                        gate(1, mod8(3, 0), 1 / ALPHA)
                    modulate(((2, 2, 2, 2, 2, 2, 2, 2, 1, 1, 0), (1, 2, 1, 2, 1, 1, 1, 1, 1, 1, 1))[l][i])
                if l == 0:
                    coefficients(2, mod8(4, 0), mod8(4, 1), pcol["ln_g"][:, 8:16], pcol["ln_b"][:, 8:16])
                else:
                    coefficients(4, mod8(7, 0), mod8(7, 1), pcol["norm_g"][:, 0:8])
                product("ffo", l, FI - 1)
                dve.wait_ge(sem("x_ready"), 8 * (2 * l + 1))
                for m in range(KT):
                    residual(2 * l + 1, m, bank[4 + m // 2][:, (m % 2) * S:(m % 2 + 1) * S])

            def log1p(dst, e, t):
                a, b = t
                link(dve.tensor_scalar(a, e, 2.0, None, ALU.add))
                link(dve.reciprocal(a, a))
                link(dve.tensor_tensor(dst, e, a, ALU.mult))
                link(dve.tensor_tensor(a, dst, dst, ALU.mult))
                link(dve.tensor_scalar(b, a, 1.0 / 15, None, ALU.mult))
                for i in (13, 11, 9, 7, 5, 3):
                    link(dve.scalar_tensor_tensor(b, b, 1.0 / i, a, ALU.add, ALU.mult))
                link(dve.scalar_tensor_tensor(dst, b, 1.0, dst, ALU.add, ALU.mult))

            def angles(dst, quarter):
                link(dve.tensor_scalar(turns, angle, 1 / (2 * np.pi), quarter, ALU.mult, ALU.add))
                link(dve.tensor_scalar(turns, turns, MAGIC, None, ALU.add))
                link(dve.tensor_scalar(turns, turns, -MAGIC, None, ALU.add))
                src = angle
                for part in TURN:
                    link(dve.scalar_tensor_tensor(dst, turns, -part, src, ALU.mult, ALU.add))
                    src = dst
                link(dve.tensor_scalar(dst, dst, quarter * 2 * np.pi, PI_DOWN, ALU.add, ALU.min))
                dve.tensor_scalar(dst, dst, -PI_DOWN, None, ALU.max).then_inc(sem("turned_angles"), 1)

            dve.memset(relb[BUCKETS:BUCKETS + 1, :], NEG).then_inc(sem("ones"), 1)
            dve.wait_ge(sem("c_act"), 1)
            modulate(3)
            dve.wait_ge(sem("pos_in"), 16 * 2)
            dve.wait_ge(sem("const_in"), 16)
            link(dve.tensor_copy(pos, pos_i))
            link(dve.tensor_copy(posq, posq_i[:, :]))
            link(dve.tensor_scalar(angle, pos, const(C_COL), None, ALU.mult))
            modulate(1)
            angles(sin, 0.0)
            modulate(2)
            angles(cos, 0.25)
            modulate(2)
            fold(0, (2, 0))
            coefficients(0, mod8(0, 0), mod8(0, 1))
            ahead(0)
            for m in range(KT + 1):
                if m < KT:
                    dve.wait_ge(sem("x_copied"), m // 2 + 1)
                    h_full(0, m, tiles(x, m, m + 1))
                if m:
                    h_low(0, m - 1)

            product("mla_in", 0)
            modulate(1)
            product("mla_in", 1)
            for j in range(2):
                if j:
                    product("mla_in", 2)
                dve.wait_ge(sem("c_rooted"), j + 1)
                link(dve.reciprocal(tiles(rstd, j, j + 1), tiles(rstd, j, j + 1)))
                g = pcol["kv_norm" if j else "q_norm"]
                for m in range(2):
                    dve.scalar_tensor_tensor(tiles(hf, 2 * j + m, 2 * j + m + 1), bank[j][:, m * S:(m + 1) * S],
                                             g[:, m:m + 1], tiles(rstd, j, j + 1), ALU.mult,
                                             ALU.mult).then_inc(sem("c_full"), 1)
            for j in range(2):
                dve.wait_ge(sem("c_hi"), j + 1)
                dve.tensor_tensor(tiles(o_lo, 2 * j, 2 * j + 2), tiles(hf, 2 * j, 2 * j + 2),
                                  tiles(o_hi, 2 * j, 2 * j + 2).bitcast(F32), ALU.subtract).then_inc(
                                      sem("c_ready"), 1)
            modulate(1)
            dve.wait_ge(sem("rotary"), 2)
            dve.wait_ge(sem("kr_spread"), 1)
            link(dve.tensor_tensor(tiles(kk, 5, 6), bank[4][:, 0:S], cos, ALU.mult))
            link(dve.tensor_tensor(tiles(kk, 6, 7), bank[4][:, S:2 * S], sin, ALU.mult))
            link(dve.tensor_tensor(tiles(kk, 7, 8), tiles(kk, 5, 6), tiles(kk, 6, 7), ALU.add))
            link(dve.tensor_scalar(tiles(of, 6, 7), tiles(kk, 7, 8), half[0], None, ALU.mult))
            dve.tensor_scalar(tiles(of, 7, 8), tiles(kk, 7, 8), half[1], None, ALU.mult).then_inc(
                sem("kr_ready"), 1)
            for j in range(2):
                product("uq", j)
                modulate(1)
                dve.wait_ge(sem("q_swapped"), j + 1)
                link(dve.tensor_tensor(grid(tiles(kk, 8, 10), 2), grid(tiles(of, 4, 6), 2), row_times(cos, 2),
                                       ALU.mult))
                link(dve.tensor_tensor(grid(tiles(kk, 10, 12), 2), grid(bank[3][:, :], 2), row_times(sin, 2),
                                       ALU.mult))
                dve.tensor_tensor(tiles(of, 2 * j, 2 * j + 2), tiles(kk, 8, 10), tiles(kk, 10, 12),
                                  ALU.add).then_inc(sem("q_rotated"), 1)
                if j == 0:
                    modulate(1)
                product("ukv", j)
                if j == 0:
                    modulate(1)
            causal = lambda t: (mask[:, 0:P], mask[:, P:CAUSAL])
            for t, (a, b) in enumerate(((0, P), (P, CAUSAL))):
                link(dve.tensor_scalar(dist[:, a:b], pos[:, 0:b - a], posq[:, t:t + 1], None, ALU.subtract))
                link(magnitude(dist[:, a:b], dist[:, a:b]))
                dve.tensor_tensor(dist[:, a:b], dist[:, a:b], mask[:, a:b], ALU.subtract).then_inc(
                    sem("dist_ready"), 1)
            attention("mla", False, unit0("mla_o", 0), (0, 2, 4, 6, 8, 10), causal)

            fold(1, (0, 1))
            gate(0, mod8(1, 0), 1 / ALPHA)

            def after_mla(i):
                if i < 2:
                    modulate(2)
                if i == 2:
                    fold(2, (0, 1))
                    coefficients(1, mod8(1, 1), mod8(2, 0), pcol["ln_g"][:, 0:8], pcol["ln_b"][:, 0:8])

            out_projection("mla_o", 0, after_mla)
            norm(0, 1)
            ffn(0)
            norm(1, 2)

            for i in range(12):
                product("moba_in", i)
                if i in (6, 7):
                    fold(5, (5, 6), (0, 1) if i == 6 else (2, 3))
                if i == 7:
                    gate(2, mod8(5, 0), 1 / ALPHA)
                if i < 11:
                    modulate(1)
            attention("moba", False, unit0("moba_o", 0), (2, 5, 8),
                      lambda t: (alibi[t % 2][:, 0:P], alibi[t % 2][:, P:CAUSAL]))
            dve.wait_ge(sem("x_ready"), 16)

            def after_moba(i):
                if i < 3:
                    modulate(1)
                if i == 2:
                    fold(6, (0, 1))
                    gate(3, mod8(6, 1), 1 / ALPHA)
                    coefficients(3, mod8(5, 1), mod8(6, 0), pcol["ln_g"][:, 16:24], pcol["ln_b"][:, 16:24])

            out_projection("moba_o", 2, after_moba)
            norm(2, 3)
            ffn(1)
            norm(3, None)
            norm(4, 4)

            link(dve.memset(rstd[:, :], 0.0))
            product("a_kv", 0)
            product("f", 0)
            dve.wait_ge(sem("turn_read"), turn_of[("f", 0)] + 1)
            v = prob[0:16, 0:S]
            magnitude(prob[0:16, S:2 * S], v).then_inc(sem("f_abs"), 1)
            fold(8, (5, 6))
            for m in range(2):
                product("a_q", m)
                modulate(1)
            gate(4, mod8(8, 0), 1.0)
            gate(5, mod8(8, 1), 1.0)
            for m in range(2):
                product("b_q", m)
                modulate(1)
            dve.wait_ge(sem("akv_turned"), 1)
            for at, src, h in ((0, tiles(kk, 8, 9), 0), (1, bank[4][:, 0:S], 1), (2, bank[4][:, 0:S], 0),
                               (3, tiles(kk, 8, 9), 1)):
                dve.tensor_scalar(tiles(kk, at, at + 1), src, half[h], None, ALU.mult).then_inc(
                    sem("akv_spread"), 1)
            dve.wait_ge(sem("vv_zero"), 1)
            for h in range(2):
                for side in range(2):
                    dst = vv[:, :].rearrange("p (t n f) -> p t n f", t=2, n=12)[:, :, 2 * h + side,
                                                                               side * 64:(side + 1) * 64]
                    src = bank[4][:, S:2 * S].rearrange("p (t f) -> p t f", t=2)[:, :, h * 64:(h + 1) * 64]
                    dve.tensor_copy(dst, src).then_inc(sem("akv_spread"), 1)
            product("b_k", 0)
            modulate(1)
            dve.wait_ge(sem("f_exp"), 1)
            q, r = prob[0:16, 3 * S:4 * S], of[0:16, 0:S]
            log1p(q, prob[0:16, 2 * S:3 * S], (prob[0:16, S:2 * S], r))
            product("b_k", 1)
            link(dve.tensor_scalar(v, v, 0.0, None, ALU.min))
            link(dve.scalar_tensor_tensor(v, q, -2.0, v, ALU.mult, ALU.add))
            link(dve.tensor_tensor_scan(rstd[0:16, 0:S], ones[0:16, 0:1].broadcast_to([16, S]), v, 0.0, ALU.mult,
                                        ALU.add))
            dve.tensor_scalar(rstd[:, S:2 * S], rstd[:, 0:S], const(C_COL + 4), const(C_COL + 5), ALU.mult,
                              ALU.add).then_inc(sem("decay_ready"), 1)
            for m in range(2):
                product("b_v", m)
            dve.wait_ge(sem("bias_in"), 16 * 8)
            dve.wait_ge(sem("attn_in"), 16 * 3)
            attention("swa", True, unit0("a_gate", 0), (),
                      lambda t: (tiles(bias, t, t + 1)[:, P:S], tiles(bias, t, t + 1)))
            for h in range(HEADS):
                dve.tensor_scalar(tiles(bias, h, h + 1), rstd[:, 0:S], const(C_SELF + h), const(C_SEL1 + h),
                                  ALU.mult, ALU.add).then_inc(sem("decay_ready"), 1)
            lam, lab, lex = pcol["lam"], small[:, 40:48], small[:, 48:56]
            magnitude(lab, lam).then_inc(sem("lam_abs"), 1)
            attention("fgt", True, unit0("a_gate", 0), (2,), causal)
            dve.wait_ge(sem("lam_exp"), 1)
            log1p(small[:, 56:64], lex, (small[:, 64:72], small[:, 72:80]))
            link(dve.tensor_scalar(small[:, 80:88], lam, -1.0, 0.0, ALU.mult, ALU.max))
            link(dve.scalar_tensor_tensor(small[:, 80:88], small[:, 56:64], 2.0, small[:, 80:88], ALU.mult, ALU.add))
            link(dve.tensor_scalar(lam8, small[:, 80:88], -LRU_C, None, ALU.mult))
            def o_low(src, m, count):
                dve.wait_ge(sem("o_hi_ready"), count + m + 1)
                dve.tensor_tensor(tiles(o_lo, 2 * m, 2 * m + 2), tiles(src, 2 * m, 2 * m + 2),
                                  tiles(o_hi, 2 * m, 2 * m + 2).bitcast(F32), ALU.subtract).then_inc(
                                      sem("o_ready"), 1)

            for m in range(5):
                if m < 4:
                    product("a_gate", m)
                    dve.wait_ge(sem("turn_read"), turn_of[("a_gate", m)] + 1)
                    dve.wait_ge(sem("pair_read"), 8)
                    dve.tensor_tensor(tiles(of, 2 * m, 2 * m + 2), tiles(of, 2 * m, 2 * m + 2),
                                      prob[:, (m % 2) * 512:(m % 2 + 1) * 512], ALU.mult).then_inc(
                                          sem("head_gated"), 1)
                if m:
                    o_low(of, m - 1, 16)

            def after_attention(i):
                if i < 2:
                    modulate(1)
                if i == 2:
                    fold(9, (0, 1))
                    coefficients(5, mod8(9, 0), mod8(9, 1), pcol["norm_g"][:, 8:16])

            out_projection("attn_o", 4, after_attention)
            norm(5, 5)

            cw = pcol["conv2_w"]

            def xc_low(m):
                dve.wait_ge(sem("xc_hi"), m + 1)
                dve.tensor_tensor(tiles(o_lo, 2 * m, 2 * m + 2), tiles(kk, 2 * m, 2 * m + 2),
                                  tiles(o_hi, 2 * m, 2 * m + 2).bitcast(F32), ALU.subtract).then_inc(
                                      sem("xc_ready"), 1)

            for m in range(4):
                product("xr", m)
                b = bank[turn_of[("xr", m)] % 4]
                for j in (2, 1, 0):
                    for t in range(2):
                        f = 2 * m + t
                        dve.wait_ge(sem("xc_started"), 2 * m + 2)
                        c, a = tiles(kk, f, f + 1), b[:, t * S:(t + 1) * S]
                        back = CONV2 - 1 - j
                        ins = dve.scalar_tensor_tensor(c[:, back:S], a[:, 0:S - back],
                                                       cw[:, 8 * j + f:8 * j + f + 1], c[:, back:S], ALU.mult,
                                                       ALU.add)
                        if j:
                            link(ins)
                        else:
                            ins.then_inc(sem("xc_full"), 1)
                dve.nop().then_inc(sem("turn_read"), 1)
                if m:
                    xc_low(m - 1)
            xc_low(3)
            product("l_gate", LRU_EARLY - 1)
            product("w_a", 0)
            for n in range(KT):
                dve.wait_ge(sem("rg_read"), n + 1)
                dve.tensor_scalar(tiles(qz, n, n + 1), tiles(qz, n, n + 1), lam8[:, n:n + 1], None,
                                  ALU.mult).then_inc(sem("rate_ready"), 1)
            product("w_x", 0)
            ahead(unit0("l_gate", LRU_EARLY) + AHEAD)
            for i in range(2):
                a, b = 4 * i, 4 * i + 4
                dve.wait_ge(sem("decay_exp"), 2 * i + 2)
                dve.scalar_tensor_tensor(tiles(of, a, b), tiles(of, a, b), 1.0, tiles(bias, a, b), ALU.add,
                                         ALU.mult).then_inc(sem("ratio_ready"), 1)
            ahead(unit0("l_gate", LRU_EARLY) + 1 + AHEAD)
            for i in range(2):
                a, b = 4 * i, 4 * i + 4
                dve.wait_ge(sem("input_root"), i + 1)
                dve.wait_ge(sem("ix_ready"), i + 1)
                link(dve.tensor_tensor(tiles(vv, a, b), tiles(vv, a, b), tiles(of, a, b), ALU.mult))
                for m in range(4 * i, 4 * i + 4):
                    dve.tensor_tensor_scan(tiles(bias, m, m + 1), tiles(qz, m, m + 1), tiles(vv, m, m + 1), 0.0,
                                           ALU.mult, ALU.add).then_inc(sem("scanned"), 1)
            for m in range(LRU_EARLY, 4):
                product("l_gate", m)
            for m in range(5):
                if m == 4:
                    o_low(kk, 3, 20)
                    continue
                dve.wait_ge(sem("turn_read"), turn_of[("l_gate", m)] + 1)
                dve.wait_ge(sem("scanned"), 2 * m + 2)
                dve.tensor_tensor(tiles(kk, 2 * m, 2 * m + 2),
                                  tiles(kk, 2 * m, 2 * m + 2) if m >= LRU_EARLY else prob[:, m * 512:(m + 1) * 512],
                                  tiles(bias, 2 * m, 2 * m + 2), ALU.mult).then_inc(sem("l_gated"), 1)
                if m:
                    o_low(kk, m - 1, 20)
            out_projection("lru_o", 5)
            norm(6, None)


INPUTS = ["x", "c", "positions", "mod_w", "mod_b", "ln_g", "ln_b", "ffn_w_in", "ffn_conv_w", "ffn_conv_b",
          "ffn_w_out", "mla_w_in", "mla_q_norm", "mla_w_uq", "mla_kv_norm", "mla_w_ukv", "mla_w_o", "moba_w_in",
          "moba_w_o", "c_2", "rel_bias_2", "norm_g_2", "ada_w_2", "ada_b_2", "attn_w_in_2", "attn_sinks_2",
          "attn_b_f_2", "attn_w_out_2", "lru_w_in_2", "lru_conv_w_2", "lru_conv_b_2", "lru_w_a_2", "lru_b_a_2",
          "lru_w_x_2", "lru_b_x_2", "lru_lambda_2", "lru_w_out_2", "final_g_2"]


def kernel(**inputs):
    import concourse.bacc as bacc
    from concourse.bass_utils import run_bass_kernel_spmd

    nc = bacc.Bacc("TRN2", target_bir_lowering=False, num_devices=1)
    arrays, w = {}, {}
    for name in INPUTS:
        a = np.ascontiguousarray(inputs[name])
        arrays[f"in_{name}"] = a
        w[name] = nc.dram_tensor(f"in_{name}", a.shape, mybir.dt.from_np(a.dtype), kind="ExternalInput").ap()
    table = constants()
    arrays["in_constants"] = table
    consts = nc.dram_tensor("in_constants", table.shape, F32, kind="ExternalInput").ap()
    out = nc.dram_tensor("out_x", (1, S, D), F32, kind="ExternalOutput").ap()
    build(nc, w, consts, out)
    r = run_bass_kernel_spmd(nc, [arrays], core_ids=[0])
    return r.results[0]["out_x"]
```
